# Optimizing a Trainium2 kernel written in Bass

```python
import math
import jax, jax.numpy as jnp
from jax import lax
import numpy as np

D_MODEL = 1024
BATCH = 1
SEQ = 512
DEPTH = 1
DEC_BATCH = 1
DEC_SEQ = 1024
PAST_LEN = 128

HEAD_DIM = 64
N_Q_A = 8
N_KV_A = 2
GROUP_A = N_Q_A // N_KV_A
N_HEADS_B = 8
WIDTH_A = N_Q_A * HEAD_DIM
WIDTH_B = N_HEADS_B * HEAD_DIM
MIX_WIDTH = WIDTH_A + WIDTH_B
KV_WIDTH_A = N_KV_A * HEAD_DIM
IN_PROJ_WIDTH = WIDTH_A + 2 * KV_WIDTH_A + 3 * WIDTH_B
Q_BLOCK = 128
GRID_W = 64
ROPE_AXIS_DIM = HEAD_DIM // 2
ROPE_THETA = 10000.0
NA_KH = 8
NA_KW = 16
D_FF = 2816
CONV_W = 3
PLE_DIM = 256
EPS = 1e-6

kernel_name = "hymba_gqa_natten_convffn_ple_encoder"

def _rmsnorm(x, g):
    x32 = x.astype(jnp.float32)
    y = x32 * lax.rsqrt(jnp.mean(x32 * x32, axis=-1, keepdims=True) + EPS)
    return (y * g.astype(jnp.float32)).astype(x.dtype)

def _rope_tables(seq):
    t = jnp.arange(seq)
    row = (t // GRID_W).astype(jnp.float32)
    col = (t % GRID_W).astype(jnp.float32)
    freqs = ROPE_THETA ** (-jnp.arange(0, ROPE_AXIS_DIM, 2, dtype=jnp.float32) / ROPE_AXIS_DIM)
    ang_r = row[:, None] * freqs[None]
    ang_c = col[:, None] * freqs[None]
    return jnp.cos(ang_r), jnp.sin(ang_r), jnp.cos(ang_c), jnp.sin(ang_c)

def _rotate(x, cos, sin):
    cos = cos[None, :, None, :].astype(x.dtype)
    sin = sin[None, :, None, :].astype(x.dtype)
    x1, x2 = jnp.split(x, 2, axis=-1)
    return jnp.concatenate([x1 * cos - x2 * sin, x2 * cos + x1 * sin], axis=-1)

def _axial_rope(x, tables):
    cos_r, sin_r, cos_c, sin_c = tables
    xr, xc = x[..., :ROPE_AXIS_DIM], x[..., ROPE_AXIS_DIM:]
    return jnp.concatenate([_rotate(xr, cos_r, sin_r), _rotate(xc, cos_c, sin_c)], axis=-1)

def _gqa_blocked(q, k, v):
    b, s, _, dh = q.shape
    nb = s // Q_BLOCK
    scale = 1.0 / math.sqrt(dh)
    qb = q.reshape(b, nb, Q_BLOCK, N_KV_A, GROUP_A, dh).transpose(1, 0, 2, 3, 4, 5)

    def block(qblk):
        sc = jnp.einsum('bqkgd,bskd->bkgqs', qblk, k, preferred_element_type=jnp.float32) * scale
        p = jax.nn.softmax(sc, axis=-1).astype(v.dtype)
        return jnp.einsum('bkgqs,bskd->bqkgd', p, v)

    o = lax.map(block, qb)
    return o.transpose(1, 0, 2, 3, 4, 5).reshape(b, s, WIDTH_A)

def _neighbourhood_attention(q, k, v, rpb):
    b, s, h, dh = q.shape
    rows = s // GRID_W
    kh = min(NA_KH, rows)
    scale = 1.0 / math.sqrt(dh)
    qg = q.reshape(b, rows, GRID_W, h, dh)
    kg = k.reshape(b, rows, GRID_W, h, dh)
    vg = v.reshape(b, rows, GRID_W, h, dh)
    r_idx = jnp.arange(rows)
    r_start = jnp.clip(r_idx - kh // 2, 0, rows - kh)
    c = jnp.arange(GRID_W)
    c_start = jnp.clip(c - NA_KW // 2, 0, GRID_W - NA_KW)
    kc = c
    col_ok = (kc[None, :] >= c_start[:, None]) & (kc[None, :] < c_start[:, None] + NA_KW)
    dc_idx = jnp.clip(kc[None, :] - c[:, None] + NA_KW - 1, 0, 2 * NA_KW - 2)
    rpb_c = rpb[:, :, dc_idx].astype(jnp.float32)

    def row_fn(args):
        r, r0, q_row = args
        k_strip = lax.dynamic_slice_in_dim(kg, r0, kh, axis=1)
        v_strip = lax.dynamic_slice_in_dim(vg, r0, kh, axis=1)
        dr_idx = r0 + jnp.arange(kh) - r + NA_KH - 1
        bias = rpb_c[:, dr_idx].transpose(0, 2, 1, 3)
        sc = jnp.einsum('bqhd,bikhd->bhqik', q_row, k_strip,
                        preferred_element_type=jnp.float32) * scale + bias[None]
        sc = jnp.where(col_ok[None, None, :, None, :], sc, -jnp.inf)
        p = jax.nn.softmax(sc.reshape(b, h, GRID_W, kh * GRID_W), axis=-1)
        p = p.reshape(b, h, GRID_W, kh, GRID_W).astype(v.dtype)
        return jnp.einsum('bhqik,bikhd->bqhd', p, v_strip)

    o = lax.map(row_fn, (r_idx, r_start, qg.transpose(1, 0, 2, 3, 4)))
    return o.transpose(1, 0, 2, 3, 4).reshape(b, s, WIDTH_B)

def _dwconv_centred(u, w, bias):
    up = jnp.pad(u, ((0, 0), (1, 1), (0, 0)))
    return up[:, :-2] * w[0] + up[:, 1:-1] * w[1] + up[:, 2:] * w[2] + bias

def _trunk(x, p, attn_norm, w_in, q_norm_a, k_norm_a, rpb_b, out_norm_a, out_norm_b,
           w_out, ffn_norm, w_up, conv_w, conv_b, w_down, ple_norm, w_ple_gate, w_ple,
           final_norm):
    b, s, _ = x.shape
    tables = _rope_tables(s)
    h = x
    for i in range(DEPTH):
        n = _rmsnorm(h, attn_norm[i])
        proj = n @ w_in[i]
        splits = np.cumsum([WIDTH_A, KV_WIDTH_A, KV_WIDTH_A, WIDTH_B, WIDTH_B])
        qa, ka, va, qb, kb, vb = jnp.split(proj, splits, axis=-1)
        qa = _rmsnorm(qa.reshape(b, s, N_Q_A, HEAD_DIM), q_norm_a[i])
        ka = _rmsnorm(ka.reshape(b, s, N_KV_A, HEAD_DIM), k_norm_a[i])
        va = va.reshape(b, s, N_KV_A, HEAD_DIM)
        qa = _axial_rope(qa, tables)
        ka = _axial_rope(ka, tables)
        out_a = _gqa_blocked(qa, ka, va)
        out_b = _neighbourhood_attention(qb.reshape(b, s, N_HEADS_B, HEAD_DIM),
                                         kb.reshape(b, s, N_HEADS_B, HEAD_DIM),
                                         vb.reshape(b, s, N_HEADS_B, HEAD_DIM), rpb_b[i])
        mixed = jnp.concatenate([_rmsnorm(out_a, out_norm_a[i]),
                                 _rmsnorm(out_b, out_norm_b[i])], axis=-1)
        h = h + mixed @ w_out[i]
        n2 = _rmsnorm(h, ffn_norm[i])
        u = _dwconv_centred(n2 @ w_up[i], conv_w[i], conv_b[i])
        a, g = jnp.split(u, 2, axis=-1)
        h = h + (a * jax.nn.gelu(g, approximate=True)) @ w_down[i]
        gate = jax.nn.sigmoid(_rmsnorm(h, ple_norm[i]) @ w_ple_gate[i])
        h = h + gate * (p[i] @ w_ple[i])
    return _rmsnorm(h, final_norm)

def setup_inputs(seed: int = 0) -> dict:
    key = jax.random.key(seed)
    ks = jax.random.split(key, 24)
    f32 = jnp.float32

    def nrm(k, shape, scale):
        return jax.random.normal(k, shape, f32) * scale

    def gain(k, shape):
        return 1.0 + 0.05 * jax.random.normal(k, shape, f32)

    return {
        "x_prompt": nrm(ks[0], (BATCH, SEQ, D_MODEL), 1.0),
        "x_sample": nrm(ks[1], (DEC_BATCH, DEC_SEQ, D_MODEL), 1.0),
        "p_prompt": nrm(ks[2], (DEPTH, BATCH, SEQ, PLE_DIM), 1.0),
        "p_sample": nrm(ks[3], (DEPTH, DEC_BATCH, DEC_SEQ, PLE_DIM), 1.0),
        "attn_norm": gain(ks[4], (DEPTH, D_MODEL)),
        "w_in": nrm(ks[5], (DEPTH, D_MODEL, IN_PROJ_WIDTH), D_MODEL ** -0.5),
        "q_norm_a": gain(ks[6], (DEPTH, HEAD_DIM)),
        "k_norm_a": gain(ks[7], (DEPTH, HEAD_DIM)),
        "rpb_b": nrm(ks[8], (DEPTH, N_HEADS_B, 2 * NA_KH - 1, 2 * NA_KW - 1), 0.1),
        "out_norm_a": gain(ks[9], (DEPTH, WIDTH_A)),
        "out_norm_b": gain(ks[10], (DEPTH, WIDTH_B)),
        "w_out": nrm(ks[11], (DEPTH, MIX_WIDTH, D_MODEL), MIX_WIDTH ** -0.5),
        "ffn_norm": gain(ks[12], (DEPTH, D_MODEL)),
        "w_up": nrm(ks[13], (DEPTH, D_MODEL, 2 * D_FF), D_MODEL ** -0.5),
        "conv_w": nrm(ks[14], (DEPTH, CONV_W, 2 * D_FF), CONV_W ** -0.5),
        "conv_b": nrm(ks[15], (DEPTH, 2 * D_FF), 0.02),
        "w_down": nrm(ks[16], (DEPTH, D_FF, D_MODEL), D_FF ** -0.5),
        "ple_norm": gain(ks[17], (DEPTH, D_MODEL)),
        "w_ple_gate": nrm(ks[18], (DEPTH, D_MODEL, D_MODEL), D_MODEL ** -0.5),
        "w_ple": nrm(ks[19], (DEPTH, PLE_DIM, D_MODEL), PLE_DIM ** -0.5),
        "final_norm": gain(ks[20], (D_MODEL,)),
    }

def reference(x_prompt, x_sample, p_prompt, p_sample, attn_norm, w_in, q_norm_a, k_norm_a,
              rpb_b, out_norm_a, out_norm_b, w_out, ffn_norm, w_up, conv_w, conv_b, w_down,
              ple_norm, w_ple_gate, w_ple, final_norm):
    y_prompt = _trunk(x_prompt, p_prompt, attn_norm, w_in, q_norm_a, k_norm_a, rpb_b,
                      out_norm_a, out_norm_b, w_out, ffn_norm, w_up, conv_w, conv_b, w_down,
                      ple_norm, w_ple_gate, w_ple, final_norm)
    y_sample = _trunk(x_sample, p_sample, attn_norm, w_in, q_norm_a, k_norm_a, rpb_b,
                      out_norm_a, out_norm_b, w_out, ffn_norm, w_up, conv_w, conv_b, w_down,
                      ple_norm, w_ple_gate, w_ple, final_norm)
    return (y_prompt, y_sample)


_drawn_inputs = setup_inputs


def setup_inputs(seed=0):
    import zlib

    import numpy as np

    out = dict(_drawn_inputs(seed))
    spreads = {}
    factors = {'conv_b': 4.965, 'ple_norm': 21.724}
    for name, (base, spread) in spreads.items():
        noise = np.random.default_rng([zlib.crc32(name.encode()), seed]).standard_normal(out[name].shape)
        drawn = base * np.exp(spread * noise) if base else spread * noise
        out[name] = __import__('jax').numpy.asarray(drawn.astype(out[name].dtype))
    for name, factor in factors.items():
        out[name] = (out[name] * factor).astype(out[name].dtype)
    return out
```

```python
from contextlib import ExitStack

import numpy as np

import concourse.bass as bass
from concourse import mybir

F32 = mybir.dt.float32
F32R = mybir.dt.float32r
ALU = mybir.AluOpType
ACT = mybir.ActivationFunctionType
AXX = mybir.AxisListType.X

P = 128
D = 1024
KT = D // P
TP, TS = 512, 1024
T = TP + TS
GT = 512
G = T // GT
DH = 64
NPAIR_A, NPAIR_B = 4, 4
NPAIR = NPAIR_A + NPAIR_B
FF = 2816
NJ = FF // P
PLE = 256
EPS = 1e-6
GRID = 64
NA_KH, NA_KW = 8, 16
RPB_R, RPB_C = 2 * NA_KH - 1, 2 * NA_KW - 1
RPB_PAD = GRID - NA_KW
NEG = 1e30
QSCALE = 1.0 / np.sqrt(DH)

N_IN = 18
N_OUT = 8
N_FF = 3 * NJ
N_PLE = 12
OUT0 = N_IN
FF0 = OUT0 + N_OUT
PLE0 = FF0 + N_FF
NW = PLE0 + N_PLE
NA_TILES = 5

ITEMS = 24


def item(m):
    s, n = divmod(m, 12)
    g, t = divmod(n, 4)
    return s, g, t, 3 * s + g


def window(kind, m):
    _, g, t, _ = item(m)
    if kind == "A":
        return (0, TP, None, 0) if g == 0 else (TP, TS, None, 0)
    rows = (TP if g == 0 else TS) // GRID
    r = 2 * (t if g == 0 else 4 * (g - 1) + t)
    first = min(max(r - NA_KH // 2, 0), rows - NA_KH)
    base = 0 if g == 0 else TP
    last = min(max(r + 1 - NA_KH // 2, 0), rows - NA_KH)
    if last > first:
        return base + first * GRID, (NA_KH + 1) * GRID, "mid", 0
    return base + first * GRID, NA_KH * GRID, "edge", first - r + NA_KH - 1


def key_blocks(width):
    return [(k, min(P, width - P * k)) for k in range(-(-width // P))]


V1_AT = 6


def uses_of(bank):
    order = [("V", 0)]
    for m in range(ITEMS):
        order.append(("T", m))
        if bank == 0 and m % 4 == 0 and m:
            order.append(("R", m // 4 - 1))
        if m == V1_AT:
            order.append(("V", 1))
    if bank == 0:
        order.append(("R", 5))
    return {name: n for n, name in enumerate(order)}


USE = [uses_of(0), uses_of(1)]
NUSE = [len(u) for u in USE]


def build(nc, a):
    ctx = ExitStack()
    with ctx:
        def sem(name):
            return ctx.enter_context(nc.semaphore(name))

        base = ((nc.sbuf_base + 31) // 32) * 32
        KB = 1024

        class Region:

            def __init__(self, at):
                self.at = at

            def __call__(self, name, shape, dt=F32):
                h = nc.alloc_sbuf_tensor_at(name, [P] + list(shape), dt, offset=self.at)
                self.at += ((int(np.prod(shape)) * 4 + 31) // 32) * 32
                return h

        c = Region(base)
        misc = c("misc", [3 + NA_TILES])
        ones_d, ones_half, eps, qk_g = misc[:, 0:1], misc[:, 1:2], misc[:, 2:3], misc[:, 3:3 + NA_TILES]
        gains = c("gains", [4, KT])
        final_g = c("final_g", [KT])
        convw = c("convw", [2 * NJ, 3])
        convb = c("convb", [2 * NJ])
        tok_std = c("tok_std", [24])
        tok_r = c("tok_r", [24])
        rsum = c("rsum", [ITEMS])
        nmax = c("nmax", [ITEMS])
        rinv = c("rinv", [2, 4])
        ident = c("ident", [P])
        squares0 = c.at
        blk = c("blk", [P])
        perm = c("perm", [P])
        colmask = c("colmask", [GRID])
        gate_t = nc.alloc_sbuf_tensor_at("gate_t", [P, GT], F32, offset=squares0)
        assert c.at <= squares0 + 2 * KB, (c.at, squares0)
        B0 = squares0 + 2 * KB

        c = Region(B0)
        NH = c("NH", [KT, T], F32R)
        NL = c("NL", [KT, T], F32R)
        WH = c("WH", [2, D], F32R)
        WL = c("WL", [2, D], F32R)
        raw = c("raw", [2, D])
        H0 = c.at
        H = c("H", [KT, T])
        X0 = c.at
        END = nc.sbuf_usable_end

        c = Region(H0)
        xst = c("xst", [KT, GT])
        sqx = c("sqx", [2, GT])
        accx = c("accx", [GT])
        rstd = c("rstd", [T])
        oa = c("oa", [T])
        ob = c("ob", [T])
        rope_c = c("rope_c", [TS])
        rope_s = c("rope_s", [TS])
        qs = c("qs", [G, GT])
        qsq = c("qsq", [2, GT])
        qstd = c("qstd", [2, GT])
        qn = c("qn", [2, GT])
        qt = c("qt", [2, GT])
        assert c.at <= END

        c = Region(B0)
        QS = [c(f"QS{s}", [T], F32R) for s in range(2)]
        KH = [c(f"KH{s}", [T], F32R) for s in range(2)]
        KL = [c(f"KL{s}", [T], F32R) for s in range(2)]
        VT = [c(f"VT{s}", [T // P, P]) for s in range(2)]
        PT = c("PT", [2, TS // P, GT])
        qraw = [c(f"qraw{s}", [T]) for s in range(2)]
        kraw = [c(f"kraw{s}", [T]) for s in range(2)]
        TM = [c(f"TM{s}", [9, GRID]) for s in range(2)]
        shared = c.at
        PRA = c("PRA", [2, TS])
        assert c.at <= H0
        c = Region(shared)
        PRB = c("PRB", [2, 9 * GRID])
        SC = c("SC", [2, 9 * GRID])
        assert c.at <= H0
        c = Region(X0)
        vraw = c("vraw", [T])
        acc_o = [c("acc_a", [T]), c("acc_b", [T])]
        sqo = c("sqo", [GT])
        rb = c("rb", [GT])
        TE = [c(f"TE{s}", [16, GRID]) for s in range(2)]
        TR = c("TR", [16, GRID])
        assert c.at <= END, (c.at, END)

        c = Region(X0)
        rstd_h = c("rstd_h", [T])
        c = Region(X0 + 18 * KB)
        to = c("to", [2, 2, GT])
        sqh = c("sqh", [2, GT])
        assert c.at <= END
        c = Region(X0 + 6 * KB)
        u = c("u", [T])
        ca = c("ca", [T])
        cg = c("cg", [T])
        MH = c("MH", [T], F32R)
        ML = c("ML", [T], F32R)
        assert c.at <= END, (c.at, END)
        c = Region(X0 + 6 * KB)
        acc_h = c("acc_h", [T])
        PH = c("PH", [2, T], F32R)
        PL = c("PL", [2, T], F32R)
        sqd = nc.alloc_sbuf_tensor_at("sqd", [P, 2, GT], F32, offset=X0 + 12 * KB)

        ps = ctx.enter_context(nc.psum_tensor("ps", [P, 8, GT], F32))

        def flat(t):
            return t.rearrange("p a b -> p (a b)")

        def at_least(eng, s, v):
            if not isinstance(v, int) or v > 0:
                eng.wait_ge(s, v)

        def cols(g, n=GT):
            return slice(g * n, (g + 1) * n)

        c_ld = sem("c_ld")
        w_ld = [sem("w_ld0"), sem("w_ld1")]
        w_sc = sem("w_sc")
        w_hi = sem("w_hi")
        w_lo = sem("w_lo")
        w_done = sem("w_done")
        stage_end = [sem(f"stage_end{k}") for k in range(4)]
        stored = sem("stored")

        def end_stage(eng, k):
            eng.drain().then_inc(stage_end[k], 1)
            eng.wait_ge(stage_end[k], 5)

        def load_weight(sp, n, slot, wait=True):
            if wait:
                at_least(sp, w_lo, n - 1)
            src = a["w"][bass.ds(n, 1)].rearrange("a p n -> p (a n)")
            nc.sync.dma_start(raw[:, slot, :], src).then_inc(w_ld[slot], 16)

        def scale_weight(pool, n, slot, which, scaled):
            pool.wait_ge(w_ld[slot], landed(n, slot))
            v = raw[:, slot, :].rearrange("p (k n) -> p k n", k=KT)
            g = gains[:, which, :].unsqueeze(2).to_broadcast([P, KT, P])
            nc.gpsimd.tensor_tensor(v, v, g, ALU.mult).then_inc(w_sc, 1)

        def landed(n, slot):
            if isinstance(n, int):
                return 16 * (n // 2 + 1)
            return (n - slot) * 8 + 16

        def split_hi(act, n, slot, scaled):
            if scaled is None:
                act.wait_ge(w_ld[slot], landed(n, slot))
            else:
                act.wait_ge(w_sc, scaled)
            at_least(act, w_done, n - 1)
            nc.scalar.activation(WH[:, slot, :], raw[:, slot, :], ACT.Copy).then_inc(w_hi, 1)

        def split_lo(dve, n, slot):
            dve.wait_ge(w_hi, n + 1)
            nc.vector.tensor_tensor(WL[:, slot, :], raw[:, slot, :], WH[:, slot, :].bitcast(F32),
                                    ALU.subtract).then_inc(w_lo, 1)

        def three_pass(out, wh, wl, xh, xl, first, last):
            nc.tensor.matmul(out, wh, xh, start=first, stop=False)
            nc.tensor.matmul(out, wh, xl, start=False, stop=False)
            return nc.tensor.matmul(out, wl, xh, start=False, stop=last)

        def project(out, slot, g, ks=range(KT)):
            for k in ks:
                mm = three_pass(out, WH[:, slot, cols(k, P)], WL[:, slot, cols(k, P)],
                                NH[:, k, cols(g)], NL[:, k, cols(g)], k == ks[0], k == ks[-1])
            return mm

        st_mm, st_std, st_r, st_bc, st_ok = (sem(f"st_{x}") for x in ("mm", "std", "r", "bc", "ok"))

        def rms_sums(pe, parts, bank):
            j = 0
            for acc, ones, n in parts:
                for i in range(n):
                    mm = nc.tensor.matmul(ps[:, bank, j:j + 1], acc[:, cols(i, P)], ones[:, 0:1], start=True, stop=True)
                    j += 1
            mm.then_inc(st_mm, 1)

        def rms_std(act, call, n, bank):
            act.wait_ge(st_mm, call)
            nc.scalar.activation(tok_std[:, 0:n], ps[:, bank, 0:n], ACT.Sqrt, bias=eps[:, 0:1]).then_inc(st_std, 1)

        def rms_recip(dve, call, n):
            dve.wait_ge(st_std, call)
            nc.vector.reciprocal(tok_r[:, 0:n], tok_std[:, 0:n]).then_inc(st_r, 1)

        def rms_spread(pe, call, b, number, bank, free=None):
            pe.wait_ge(st_r, call)
            if free is not None:
                pe.wait_ge(st_ok, free)
            for j in range(4):
                col = tok_r[:, 4 * b + j:4 * b + j + 1].to_broadcast([P, P])
                mm = nc.tensor.transpose(ps[:, bank, cols(j, P)], col, ident[:, :])
            mm.then_inc(st_bc, 1)

        def rms_row(act, number, bank, dst):
            act.wait_ge(st_bc, number)
            nc.scalar.activation(dst, ps[:, bank, :], ACT.Copy).then_inc(st_ok, 1)

        x_ld = [sem(f"x_ld{k}") for k in range(KT)]
        x_sq, x_acc, x_hi, x_lo = (sem(f"x_{x}") for x in ("sq", "acc", "hi", "lo"))
        p_rdy = sem("p_rdy")
        a_ev, b_ev = sem("a_ev"), sem("b_ev")
        q_sq, q_mean, q_std, q_rec, q_n, q_rot, q_part, q_fin = (
            sem(f"q_{x}") for x in ("sq", "mean", "std", "rec", "n", "rot", "part", "fin"))
        st_a, st_b = sem("st_a"), sem("st_b")
        BODIES = N_IN // 2

        def group_ready(eng, n, g):
            if g < 2:
                eng.wait_ge(p_rdy, 2 * n + g + 1)
            else:
                eng.wait_ge(w_done, n + 1)

        def signal_group(mm, g):
            mm.then_inc(p_rdy if g < 2 else w_done, 1)

        def s1_sync(sp):
            consts = [(ident, "ident"), (blk, "blk"), (perm, "perm"), (colmask, "colmask"), (ones_d, "ones_d"),
                      (ones_half, "ones_half"), (eps, "eps"), (gains, "gains"), (final_g, "final_g"), (qk_g, "qk_g"),
                      (convw, "convw"), (convb, "convb"), (rope_c, "rope_c"), (rope_s, "rope_s")]

            def load_x(g, k):
                at_least(sp, x_lo, KT * (g - 1) + k + 1)
                nc.sync.dma_start(xst[:, k, :], a["xT"][cols(k, P), cols(g)]).then_inc(x_ld[k], 16)

            for k in range(KT):
                load_x(0, k)
            load_weight(sp, 0, 0, wait=False)
            for t, name in consts:
                v = t[:] if len(t.shape) == 2 else flat(t[:])
                nc.sync.dma_start(v, a[name]).then_inc(c_ld, 16)
            load_weight(sp, 1, 1, wait=False)
            for g in (1, 2):
                for k in range(KT):
                    load_x(g, k)

            def body(i, head):
                load_weight(sp, i * 2 + 2, 0)
                load_weight(sp, i * 2 + 3, 1)
                first = i if head else i * 2
                second = i + NA_TILES if head else i * 2 + 1
                sp.wait_ge(q_fin if head else a_ev, (i + 1) * 3)
                nc.sync.dma_start(a["qkv"][bass.ds(first, 1)].rearrange("a p n -> p (a n)"), oa[:]).then_inc(st_a, 16)
                sp.wait_ge(b_ev, (i + 1) * 3)
                nc.sync.dma_start(a["qkv"][bass.ds(second, 1)].rearrange("a p n -> p (a n)"), ob[:]).then_inc(st_b, 16)

            with sp.Fori(0, NA_TILES) as i:
                body(i, True)
            with sp.Fori(NA_TILES, BODIES - 1) as i:
                body(i, False)
            i = BODIES - 1
            sp.wait_ge(a_ev, 3 * (i + 1))
            nc.sync.dma_start(a["qkv"][2 * i], oa[:]).then_inc(st_a, 16)
            sp.wait_ge(b_ev, 3 * (i + 1))
            nc.sync.dma_start(a["qkv"][2 * i + 1], ob[:]).then_inc(st_b, 16)
            sp.wait_ge(st_a, 16 * BODIES)
            sp.wait_ge(st_b, 16 * BODIES)

        NCONST = 14

        def s1_pool(pool):
            pool.wait_ge(c_ld, 16 * NCONST)
            scale_weight(pool, 0, 0, 0, 1)
            for g in range(G):
                for k in range(1, KT):
                    pool.wait_ge(x_sq, KT * g + k + 1)
                    if k == 1:
                        if g:
                            pool.wait_ge(st_mm, g)
                        ins = nc.gpsimd.tensor_tensor(accx[:], sqx[:, 0, :], sqx[:, 1, :], ALU.add)
                    else:
                        pool.wait_ge(x_acc, (KT - 1) * g + k - 1)
                        ins = nc.gpsimd.tensor_tensor(accx[:], accx[:], sqx[:, k % 2, :], ALU.add)
                    ins.then_inc(x_acc, 1)
                if g == 0:
                    scale_weight(pool, 1, 1, 0, 2)
            with pool.Fori(0, BODIES - 1) as i:
                scale_weight(pool, i * 2 + 2, 0, 0, i * 2 + 3)
                scale_weight(pool, i * 2 + 3, 1, 0, i * 2 + 4)

        def s1_tensor(pe):
            pe.wait_ge(c_ld, 16 * NCONST)

            def sums(g):
                pe.wait_ge(x_acc, (KT - 1) * (g + 1))
                rms_sums(pe, [(accx, ones_d, 4)], 4)

            def spread(g):
                rms_spread(pe, g + 1, 0, g + 1, 5, g if g else None)

            def main(i, g, second):
                n = i * 2 + second
                if g == 0:
                    pe.wait_ge(w_lo, n + 1)
                at_least(pe, b_ev if second else a_ev, (i - 1) * 3 + g + 1)
                signal_group(project(ps[:, 3 * second + g, :], second, g), g)

            def mean(i, g):
                pe.wait_ge(q_sq, i * 3 + g + 1)
                at_least(pe, q_std, i * 3 + g)
                nc.tensor.matmul(ps[:, 6, :], blk[:], qsq[:, g % 2, :], start=True, stop=True).then_inc(q_mean, 1)

            def rot(i, g):
                pe.wait_ge(q_n, i * 3 + g + 1)
                at_least(pe, q_part, (i * 3 + g) * 2)
                nc.tensor.matmul(ps[:, 7, :], perm[:], qn[:, g % 2, :], start=True, stop=True).then_inc(q_rot, 1)

            def body(i, first=False):
                for g in range(G):
                    if first:
                        sums(g)
                        pe.wait_ge(x_lo, KT * (g + 1))
                    main(i, g, 0)
                    if first:
                        spread(g)
                    if g == 1:
                        mean(i, 0)
                mean(i, 1)
                rot(i, 0)
                if first:
                    pe.wait_ge(st_ok, G)
                main(i, 0, 1)
                mean(i, 2)
                rot(i, 1)
                main(i, 1, 1)
                rot(i, 2)
                main(i, 2, 1)

            body(0, True)
            with pe.Fori(1, NA_TILES) as i:
                body(i)
            with pe.Fori(NA_TILES, BODIES) as i:
                for second in range(2):
                    for g in range(G):
                        main(i, g, second)

        def s1_scalar(act):
            act.wait_ge(c_ld, 16 * NCONST)
            split_hi(act, 0, 0, 1)

            def x_split(g):
                for k in range(KT):
                    act.wait_ge(x_ld[k], 16 * (g + 1))
                    at_least(act, x_acc, (KT - 1) * g + k - 2 if k > 2 else (KT - 1) * g + (k == 2))
                    nc.scalar.activation(sqx[:, k % 2, :], xst[:, k, :], ACT.Square).then_inc(x_sq, 1)
                    nc.scalar.activation(NH[:, k, cols(g)], xst[:, k, :], ACT.Copy).then_inc(x_hi, 1)

            def square(i, g):
                act.wait_ge(a_ev, i * 3 + g + 1)
                at_least(act, q_mean, i * 3 + (0, -1, 1)[g])
                nc.scalar.activation(qsq[:, g % 2, :], qs[:, g, :], ACT.Square).then_inc(q_sq, 1)

            def std(i, g):
                act.wait_ge(q_mean, i * 3 + g + 1)
                at_least(act, q_n, i * 3 + (0, -1, 1)[g])
                nc.scalar.activation(qstd[:, g % 2, :], ps[:, 6, :], ACT.Sqrt, bias=eps[:, 0:1]).then_inc(q_std, 1)

            def row(g):
                rms_row(act, g + 1, 5, rstd[:, cols(g)])

            x_split(0)
            split_hi(act, 1, 1, 2)
            rms_std(act, 1, 4, 4)
            x_split(1)
            row(0)
            rms_std(act, 2, 4, 4)
            x_split(2)
            square(0, 0)
            row(1)
            square(0, 1)
            std(0, 0)
            rms_std(act, 3, 4, 4)
            row(2)
            square(0, 2)
            std(0, 1)
            split_hi(act, 2, 0, 3)
            std(0, 2)
            with act.Fori(1, NA_TILES) as i:
                split_hi(act, i * 2 + 1, 1, i * 2 + 2)
                square(i, 0)
                square(i, 1)
                std(i, 0)
                square(i, 2)
                std(i, 1)
                split_hi(act, i * 2 + 2, 0, i * 2 + 3)
                std(i, 2)
            with act.Fori(NA_TILES, BODIES - 1) as i:
                split_hi(act, i * 2 + 1, 1, i * 2 + 2)
                split_hi(act, i * 2 + 2, 0, i * 2 + 3)
            split_hi(act, N_IN - 1, 1, N_IN)

        def s1_vector(dve):
            dve.wait_ge(c_ld, 16 * NCONST)
            split_lo(dve, 0, 0)

            def x_low(g):
                for k in range(KT):
                    dve.wait_ge(x_hi, KT * g + k + 1)
                    nc.vector.tensor_tensor(NL[:, k, cols(g)], xst[:, k, :], NH[:, k, cols(g)].bitcast(F32),
                                            ALU.subtract).then_inc(x_lo, 1)

            def out_a(i, g):
                group_ready(dve, i * 2, g)
                nc.vector.tensor_tensor(qs[:, g, :], ps[:, g, :], rstd[:, cols(g)], ALU.mult).then_inc(a_ev, 1)

            def head_norm(i, g):
                k = i * 3 + g
                dve.wait_ge(q_std, k + 1)
                nc.vector.reciprocal(qstd[:, g % 2, :], qstd[:, g % 2, :]).then_inc(q_rec, 1)
                dve.wait_ge(q_rec, k + 1)
                nc.vector.scalar_tensor_tensor(qn[:, g % 2, :], qs[:, g, :], qk_g[:, bass.ds(i, 1)], qstd[:, g % 2, :],
                                               ALU.mult, ALU.mult).then_inc(q_n, 1)

            def rotary(i, g):
                k = i * 3 + g
                tab = cols(max(g - 1, 0))
                dve.wait_ge(q_n, k + 1)
                at_least(dve, q_fin, k)
                nc.vector.tensor_tensor(qt[:, 0, :], qn[:, g % 2, :], rope_c[:, tab], ALU.mult).then_inc(q_part, 1)
                dve.wait_ge(q_rot, k + 1)
                nc.vector.tensor_tensor(qt[:, 1, :], ps[:, 7, :], rope_s[:, tab], ALU.mult).then_inc(q_part, 1)
                dve.wait_ge(q_part, k * 2 + 2)
                if g == 0:
                    dve.wait_ge(st_a, i * 16)
                nc.vector.tensor_tensor(oa[:, cols(g)], qt[:, 0, :], qt[:, 1, :], ALU.add).then_inc(q_fin, 1)

            def out_plain(i, g, second):
                group_ready(dve, i * 2 + second, g)
                if g == 0:
                    dve.wait_ge(st_b if second else st_a, i * 16)
                dst = ob if second else oa
                nc.vector.tensor_tensor(dst[:, cols(g)], ps[:, 3 * second + g, :], rstd[:, cols(g)],
                                        ALU.mult).then_inc(b_ev if second else a_ev, 1)

            def tail(i):
                head_norm(i, 1)
                rotary(i, 0)
                out_plain(i, 0, 1)
                head_norm(i, 2)
                rotary(i, 1)
                out_plain(i, 1, 1)
                rotary(i, 2)
                out_plain(i, 2, 1)

            x_low(0)
            split_lo(dve, 1, 1)
            rms_recip(dve, 1, 4)
            x_low(1)
            dve.wait_ge(st_ok, 1)
            out_a(0, 0)
            rms_recip(dve, 2, 4)
            x_low(2)
            dve.wait_ge(st_ok, 2)
            out_a(0, 1)
            rms_recip(dve, 3, 4)
            head_norm(0, 0)
            dve.wait_ge(st_ok, 3)
            out_a(0, 2)
            split_lo(dve, 2, 0)
            tail(0)
            with dve.Fori(1, NA_TILES) as i:
                split_lo(dve, i * 2 + 1, 1)
                out_a(i, 0)
                out_a(i, 1)
                head_norm(i, 0)
                out_a(i, 2)
                split_lo(dve, i * 2 + 2, 0)
                tail(i)
            with dve.Fori(NA_TILES, BODIES - 1) as i:
                split_lo(dve, i * 2 + 1, 1)
                for g in range(G):
                    out_plain(i, g, 0)
                split_lo(dve, i * 2 + 2, 0)
                for g in range(G):
                    out_plain(i, g, 1)
            split_lo(dve, N_IN - 1, 1)
            for second in range(2):
                for g in range(G):
                    out_plain(BODIES - 1, g, second)

        q_ld, k_ld, v_ld, t_ld, stk_hi, stk_lo, tab = (
            [sem(f"{x}{s}") for s in range(2)] for x in ("q_ld", "k_ld", "v_ld", "t_ld", "stk_hi", "stk_lo", "tab"))
        zeroed, pe_passed, dve_passed = sem("zeroed"), sem("pe_passed"), sem("dve_passed")
        s_rdy, m_done, e_done = sem("s_rdy"), sem("m_done"), sem("e_done")
        t_rdy = [sem("t0_rdy"), sem("t1_rdy")]
        t_free = [sem("t0_free"), sem("t1_free")]
        ri_ok, rb_ok, pv_done, o_done, o_sq, o_acc = (
            sem(x) for x in ("ri_ok", "rb_ok", "pv_done", "o_done", "o_sq", "o_acc"))
        E_FREE, PV_FREE, O_FREE, T_FREE, ACC_O_FREE, TAB_FREE = 2, 2, 2, 1, 1, 1
        TBANK, PVBANK = 4, 6
        QROW = {"A": lambda i: (i, 4, 5), "B": lambda i: (i * 3 + 6, i * 3 + 7, i * 3 + 8)}

        def probs(kind, m, w):
            return (PRA if kind == "A" else PRB)[:, m % 2, 0:w]

        def score_bank(m, w):
            return flat(ps[:, 2 * (m % 2):2 * (m % 2) + 2, :])[:, 0:w]

        def split_blocks(w):
            b = key_blocks(w)
            h = len(b) // 2
            return [b[:h] + b[2 * h:], b[h:2 * h]]

        def used(bank, p, name):
            return p * NUSE[bank] + USE[bank][name] + 1

        def s2_sync(sp):
            def load(kind, p, i, s, first=False):
                q, k, v = QROW[kind](i)
                rows = cols(s, DH)
                if not first:
                    sp.wait_ge(stk_lo[s], p * 2)
                for half in range(2):
                    src = a["qkv"][bass.ds(q, 1), rows, :].rearrange("a p n -> p (a n)")
                    nc.sync.dma_start(qraw[s][cols(half, DH), :], src).then_inc(q_ld[s], 16)
                for half in range(2):
                    src = a["qkv"][bass.ds(k, 1), rows, :].rearrange("a p n -> p (a n)")
                    nc.sync.dma_start(kraw[s][cols(half, DH), :], src).then_inc(k_ld[s], 16)
                if not first:
                    sp.wait_ge(t_rdy[1], used(1, p - 1, ("V", s)))
                src = a["qkv"][bass.ds(v, 1), rows, :].rearrange("a p n -> p (a n)")
                nc.sync.dma_start(vraw[rows, :], src).then_inc(v_ld[s], 16)
                if kind == "B":
                    sp.wait_ge(tab[1 - s], i * 3 + s + TAB_FREE)
                    for half in range(2):
                        src = bass.AP(tensor=a["rpb_tensor"], offset=(i * 2 + s) * (RPB_R * RPB_C),
                                      ap=[[1, GRID], [RPB_C, RPB_R], [1, GRID]])
                        nc.sync.dma_start(TR[cols(half, GRID), half:half + RPB_R, :], src).then_inc(t_ld[s], 16)

            for s in range(2):
                load("A", 0, 0, s, first=True)
            with sp.Fori(1, NPAIR_A) as i:
                for s in range(2):
                    load("A", i, i, s)
            with sp.Fori(0, NPAIR_B) as i:
                for s in range(2):
                    load("B", i + NPAIR_A, i, s)

        def s2_pool(pool):
            pool.sem_inc(e_done, E_FREE)
            pool.sem_inc(pv_done, PV_FREE)
            pool.sem_inc(o_done, O_FREE)
            pool.sem_inc(o_acc, ACC_O_FREE)
            for b in range(2):
                pool.sem_inc(t_free[b], T_FREE)
                pool.sem_inc(tab[b], TAB_FREE)
            for s in range(2):
                for n, (v, value) in enumerate(((VT[s][:, :, cols(1 - s, DH)], 0.0), (TM[s][GRID:P, 0, :], NEG),
                                                (TM[s][0:GRID, NA_KH, :], NEG), (acc_o[s][:], 0.0))):
                    at_least(pool, zeroed, 4 * s + n)
                    nc.gpsimd.memset(v, value).then_inc(zeroed, 1)
            pool.wait_ge(zeroed, 8)

            def body(half, p):
                for b in range(6):
                    s, g = divmod(b, 3)
                    pool.wait_ge(o_sq, p * 6 + b + 1)
                    pool.wait_ge(o_acc, p * 6 + b + ACC_O_FREE)
                    v = acc_o[half][cols(s, DH), cols(g)]
                    nc.gpsimd.tensor_tensor(v, v, sqo[cols(s, DH), :], ALU.add).then_inc(o_acc, 1)

            with pool.Fori(0, NPAIR_A) as i:
                body(0, i)
            with pool.Fori(NPAIR_A, NPAIR) as i:
                body(1, i)

        def s2_tensor(pe):
            def values(p, s):
                pe.wait_ge(v_ld[s], (p + 1) * 16)
                for b in range(2):
                    pe.wait_ge(t_free[b], used(b, p, ("V", s)) - 1 + T_FREE)
                    pe.sem_inc(pe_passed, 1)
                    for j in range(6):
                        mm = nc.tensor.transpose(ps[:, TBANK + b, cols(j, DH)], vraw[cols(s, DH), cols(6 * b + j, P)],
                                                 ident[cols(s, DH), cols(s, DH)])
                    mm.then_inc(t_rdy[b], 1)

            def scores(kind, p, m):
                s, g, t, _ = item(m)
                k0, w, _, _ = window(kind, m)
                if m % 12 == 0:
                    pe.wait_ge(stk_lo[s], p * 2 + 2)
                if kind == "A" or m < 2:
                    pe.wait_ge(e_done, p * ITEMS + m - 2 + 1 + E_FREE)
                else:
                    pe.wait_ge(m_done, p * ITEMS + m - 2 + 1)
                q = QS[s][:, g * GT + t * P:g * GT + (t + 1) * P]
                for c0 in range(0, w, GT):
                    n = min(GT, w - c0)
                    out = ps[:, 2 * (m % 2) + c0 // GT, 0:n]
                    nc.tensor.matmul(out, q, KH[s][:, k0 + c0:k0 + c0 + n], start=True, stop=False)
                    mm = nc.tensor.matmul(out, q, KL[s][:, k0 + c0:k0 + c0 + n], start=False, stop=True)
                mm.then_inc(s_rdy, 1)

            def turn(kind, p, m):
                _, w, _, _ = window(kind, m)
                pe.wait_ge(e_done, p * ITEMS + m + 1 + E_FREE)
                for b, blocks in enumerate(split_blocks(w)):
                    pe.wait_ge(t_free[b], used(b, p, ("T", m)) - 1 + T_FREE)
                    for j, (kb, kn) in enumerate(blocks):
                        src = probs(kind, m, w)[:, kb * P:kb * P + kn]
                        mm = nc.tensor.transpose(ps[0:kn, TBANK + b, cols(j, P)], src, ident[:, :])
                    mm.then_inc(t_rdy[b], 1)

            def norm_row(p, b):
                pe.wait_ge(ri_ok, p * 6 + b + 1)
                pe.wait_ge(t_free[0], used(0, p, ("R", b)) - 1 + T_FREE)
                for t in range(4):
                    mm = nc.tensor.transpose(ps[:, TBANK, cols(t, P)], rinv[:, b % 2, t:t + 1].to_broadcast([P, P]),
                                             ident[:, :])
                mm.then_inc(t_rdy[0], 1)

            def turned(p, m):
                for b in range(2):
                    pe.wait_ge(t_free[b], used(b, p, ("T", m)) + T_FREE)

            def weigh_block(p, b, part, parts):
                s, g = divmod(b, 3)
                k0, w, _, _ = window("A", 4 * b)
                n = w // P
                if part == 0:
                    turned(p, 4 * b + 3)
                    pe.wait_ge(o_done, p * 6 + b - 2 + 1 + O_FREE)
                for kb in range(part * n // parts, (part + 1) * n // parts):
                    mm = nc.tensor.matmul(ps[:, PVBANK + b % 2, :], VT[s][:, k0 // P + kb, :], PT[:, b % 2, kb, :],
                                          start=(kb == 0), stop=(kb == n - 1))
                if part == parts - 1:
                    mm.then_inc(pv_done, 1)

            def weigh_item(p, m):
                s, g, t, b = item(m)
                k0, w, _, _ = window("B", m)
                turned(p, m)
                if t == 0:
                    pe.wait_ge(o_done, p * 6 + b - 2 + 1 + O_FREE)
                blocks = key_blocks(w)
                for kb, kn in blocks:
                    mm = nc.tensor.matmul(ps[:, PVBANK + b % 2, cols(t, P)], VT[s][0:kn, k0 // P + kb, :],
                                          PT[0:kn, b % 2, kb, cols(t, P)], start=(kb == 0), stop=(kb == len(blocks) - 1))
                if t == 3:
                    mm.then_inc(pv_done, 1)

            def body(kind, p):
                values(p, 0)
                scores(kind, p, 0)
                for m in range(ITEMS):
                    if m + 1 < ITEMS:
                        scores(kind, p, m + 1)
                    turn(kind, p, m)
                    if m % 4 == 0 and m:
                        norm_row(p, m // 4 - 1)
                    if m == V1_AT:
                        values(p, 1)
                    if kind == "A" and m >= 4:
                        weigh_block(p, m // 4 - 1, m % 4, 4)
                    if kind == "B" and m:
                        weigh_item(p, m - 1)
                norm_row(p, 5)
                if kind == "A":
                    weigh_block(p, 5, 0, 1)
                else:
                    weigh_item(p, ITEMS - 1)

            pe.wait_ge(zeroed, 8)
            with pe.Fori(0, NPAIR_A) as i:
                body("A", i)
            with pe.Fori(NPAIR_A, NPAIR) as i:
                body("B", i)

        def s2_scalar(act):
            def stack(p, s, key):
                act.wait_ge((k_ld if key else q_ld)[s], (p + 1) * 32)
                at_least(act, s_rdy, p * ITEMS + 1 if s else p * ITEMS - 12)
                dst, src = (KH, kraw) if key else (QS, qraw)
                nc.scalar.activation(dst[s][:], src[s][:], ACT.Copy, scale=1.0 if key else -QSCALE).then_inc(stk_hi[s], 1)

            def values(p, s):
                act.wait_ge(t_rdy[0], used(0, p, ("V", s)))
                src = ps[:, TBANK, 0:6 * DH].rearrange("p (a c) -> p a c", c=DH)
                nc.scalar.activation(VT[s][:, 0:6, cols(s, DH)], src, ACT.Copy).then_inc(t_free[0], 1)

            def exps(kind, p, m):
                _, w, _, _ = window(kind, m)
                act.wait_ge(m_done, p * ITEMS + m + 1)
                src = score_bank(m, w) if kind == "A" else SC[:, m % 2, 0:w]
                if m >= 2:
                    act.wait_ge(t_rdy[1], used(1, p, ("T", m - 2)))
                else:
                    act.wait_ge(t_free[1], p * NUSE[1] + T_FREE)
                nc.scalar.activation(probs(kind, m, w), src, ACT.Exp, bias=nmax[:, m:m + 1], scale=-1.0,
                                     accum_out=rsum[:, m:m + 1]).then_inc(e_done, 1)

            def turned(kind, p, m):
                _, _, t, b = item(m)
                _, w, _, _ = window(kind, m)
                act.wait_ge(t_rdy[0], used(0, p, ("T", m)))
                act.wait_ge(pv_done, p * 6 + b - 2 + 1 + PV_FREE)
                blocks = split_blocks(w)[0]
                full = [x for x in blocks if x[1] == P]
                dst = PT[:, b % 2, full[0][0]:full[-1][0] + 1, cols(t, P)]
                src = ps[:, TBANK, 0:P * len(full)].rearrange("p (a c) -> p a c", c=P)
                ins = nc.scalar.activation(dst, src, ACT.Copy)
                if len(full) < len(blocks):
                    kb, kn = blocks[-1]
                    ins = nc.scalar.activation(PT[0:kn, b % 2, kb, cols(t, P)], ps[0:kn, TBANK, cols(len(full), P)], ACT.Copy)
                ins.then_inc(t_free[0], 1)

            def norm_row(p, b):
                act.wait_ge(t_rdy[0], used(0, p, ("R", b)))
                act.wait_ge(o_done, p * 6 + b + O_FREE)
                nc.scalar.activation(rb[:], ps[:, TBANK, :], ACT.Copy).then_inc(t_free[0], 1)

            def square(p, b):
                s, g = divmod(b, 3)
                act.wait_ge(o_done, p * 6 + b + 1 + O_FREE)
                act.wait_ge(o_acc, p * 6 + b + ACC_O_FREE)
                src = H[cols(s, DH), bass.ds(p, 1), cols(g)].rearrange("p a n -> p (a n)")
                nc.scalar.activation(sqo[cols(s, DH), :], src, ACT.Square).then_inc(o_sq, 1)

            def body(kind, p, last=False):
                values(p, 0)
                exps(kind, p, 0)
                for m in range(ITEMS):
                    if m + 1 < ITEMS:
                        exps(kind, p, m + 1)
                    turned(kind, p, m)
                    if m % 4 == 0 and m:
                        norm_row(p, m // 4 - 1)
                    if m == V1_AT:
                        values(p, 1)
                    if m % 4 == 1 and m >= 9:
                        square(p, m // 4 - 2)
                    if m in (1, 2):
                        stack(p, 1, m == 2)
                    if m in (14, 15) and not last:
                        stack(p + 1, 0, m == 15)
                norm_row(p, 5)
                square(p, 4)
                square(p, 5)

            act.wait_ge(zeroed, 8)
            stack(0, 0, False)
            stack(0, 0, True)
            with act.Fori(0, NPAIR_A) as i:
                body("A", i)
            with act.Fori(NPAIR_A, NPAIR - 1) as i:
                body("B", i)
            body("B", NPAIR - 1, last=True)

        def s2_vector(dve):
            def stack(p, s, key):
                dve.wait_ge(stk_hi[s], p * 2 + 1 + key)
                if key:
                    nc.vector.tensor_tensor(KL[s][:], kraw[s][:], KH[s][:].bitcast(F32), ALU.subtract).then_inc(stk_lo[s], 1)
                else:
                    v = QS[s][DH:P, :]
                    nc.vector.scalar_tensor_tensor(v, qraw[s][DH:P, :], -QSCALE, v.bitcast(F32), ALU.mult,
                                                   ALU.subtract).then_inc(stk_lo[s], 1)

            def table(i, s):
                dve.wait_ge(t_ld[s], (i + 1) * 32)
                mirrored = bass.AP(tensor=TR, offset=GRID + GRID - 1, ap=[[16 * GRID, P], [GRID, 14], [-1, GRID]])
                nc.vector.scalar_tensor_tensor(TE[s][:, 1:15, :], mirrored, -1.0, colmask[:].unsqueeze(1).to_broadcast([P, 14, GRID]), ALU.mult,
                                               ALU.add).then_inc(tab[s], 1)
                dve.wait_ge(tab[s], i * 3 + 1 + TAB_FREE)
                nc.vector.tensor_copy(TM[s][0:GRID, 0:NA_KH, :], TE[s][0:GRID, 3:3 + NA_KH, :]).then_inc(tab[s], 1)
                nc.vector.tensor_copy(TM[s][GRID:P, 1:NA_KH + 1, :], TE[s][GRID:P, 4:4 + NA_KH, :]).then_inc(tab[s], 1)
                dve.wait_ge(tab[s], i * 3 + 3 + TAB_FREE)

            def values(p, s):
                dve.wait_ge(t_rdy[1], used(1, p, ("V", s)))
                src = ps[:, TBANK + 1, 0:6 * DH].rearrange("p (a c) -> p a c", c=DH)
                nc.vector.tensor_copy(VT[s][:, 6:12, cols(s, DH)], src).then_inc(t_free[1], 1)

            def row_max(kind, p, m):
                s, g, t, _ = item(m)
                _, w, which, r0 = window(kind, m)
                dve.wait_ge(s_rdy, p * ITEMS + m + 1)
                if kind == "A":
                    nc.vector.tensor_reduce(nmax[:, m:m + 1], score_bank(m, w), AXX, ALU.min).then_inc(m_done, 1)
                else:
                    dve.wait_ge(e_done, p * ITEMS + m - 2 + 1 + E_FREE)
                    dve.sem_inc(dve_passed, 1)
                    table_rows = flat((TM if which == "mid" else TE)[s][:, r0:r0 + w // GRID, :])
                    nc.vector.tensor_tensor_reduce(out=SC[:, m % 2, 0:w], in0=score_bank(m, w), in1=table_rows, scale=1.0,
                                                   scalar=3e38, op0=ALU.add, op1=ALU.min,
                                                   accum_out=nmax[:, m:m + 1]).then_inc(m_done, 1)

            def turned(kind, p, m):
                _, _, t, b = item(m)
                _, w, _, _ = window(kind, m)
                dve.wait_ge(t_rdy[1], used(1, p, ("T", m)))
                dve.wait_ge(pv_done, p * 6 + b - 2 + 1 + PV_FREE)
                blocks = split_blocks(w)[1]
                src = ps[:, TBANK + 1, 0:P * len(blocks)].rearrange("p (a c) -> p a c", c=P)
                nc.vector.tensor_copy(PT[:, b % 2, blocks[0][0]:blocks[-1][0] + 1, cols(t, P)], src).then_inc(t_free[1], 1)

            def inverse(p, b):
                dve.wait_ge(e_done, p * ITEMS + 4 * b + 4 + E_FREE)
                nc.vector.reciprocal(rinv[:, b % 2, :], rsum[:, 4 * b:4 * b + 4]).then_inc(ri_ok, 1)

            def out(p, b):
                s, g = divmod(b, 3)
                dve.wait_ge(pv_done, p * 6 + b + 1 + PV_FREE)
                dve.wait_ge(t_free[0], used(0, p, ("R", b)) + T_FREE)
                dst = H[cols(s, DH), bass.ds(p, 1), cols(g)].rearrange("p a n -> p (a n)")
                nc.vector.tensor_tensor(dst, ps[cols(s, DH), PVBANK + b % 2, :], rb[cols(s, DH), :],
                                        ALU.mult).then_inc(o_done, 1)

            def body(kind, p, i, last=False):
                values(p, 0)
                if kind == "B":
                    table(i, 0)
                row_max(kind, p, 0)
                for m in range(ITEMS):
                    if m + 1 < ITEMS:
                        if kind == "B" and m + 1 == 12:
                            table(i, 1)
                        row_max(kind, p, m + 1)
                    if m % 4 == 0 and m >= 8:
                        out(p, m // 4 - 2)
                    turned(kind, p, m)
                    if m % 4 == 3:
                        inverse(p, m // 4)
                    if m == V1_AT:
                        values(p, 1)
                    if m in (1, 2):
                        stack(p, 1, m == 2)
                    if m in (14, 15) and not last:
                        stack(p + 1, 0, m == 15)
                out(p, 4)
                out(p, 5)

            dve.wait_ge(zeroed, 8)
            stack(0, 0, False)
            stack(0, 0, True)
            with dve.Fori(0, NPAIR_A) as i:
                body("A", i, i)
            with dve.Fori(0, NPAIR_B - 1) as i:
                body("B", i + NPAIR_A, i)
            body("B", NPAIR - 1, NPAIR_B - 1, last=True)

        oh_hi, oh_lo, r_free, r_t, r_s, h_up, h_sq, h_acc, acc_zero = (
            sem(x) for x in ("oh_hi", "oh_lo", "r_free", "r_t", "r_s", "h_up", "h_sq", "h_acc", "acc_zero"))
        o_rdy = sem("o_rdy")

        def s3_sync(sp):
            load_weight(sp, OUT0, 0)
            load_weight(sp, OUT0 + 1, 1)
            for k in range(KT):
                sp.wait_ge(oh_lo, (G - 1) * KT + k + 1)
                nc.sync.dma_start(H[:, k, :], a["xT"][cols(k, P), :]).then_inc(x_ld[k], 16)
            with sp.Fori(0, N_OUT // 2) as i:
                load_weight(sp, i * 2 + (OUT0 + 2), 0)
                load_weight(sp, i * 2 + (OUT0 + 3), 1)

        def s3_pool(pool):
            pool.sem_inc(h_acc, 1)
            nc.gpsimd.memset(rstd_h[:], 0.0).then_inc(acc_zero, 1)
            scale_weight(pool, OUT0, 0, 1, OUT0 + 1)
            scale_weight(pool, OUT0 + 1, 1, 1, OUT0 + 2)
            pool.wait_ge(acc_zero, 1)

            def body(i, last=False):
                for second in range(2):
                    if not last:
                        scale_weight(pool, i * 2 + (OUT0 + 2 + second), second, 1, None)
                    for g in range(G):
                        c = i * 6 + (3 * second + g)
                        pool.wait_ge(h_sq, c + 1)
                        pool.wait_ge(h_acc, c + 1)
                        nc.gpsimd.tensor_tensor(rstd_h[:, cols(g)], rstd_h[:, cols(g)], sqh[:, (3 * second + g) % 2, :],
                                                ALU.add).then_inc(h_acc, 1)

            with pool.Fori(0, N_OUT // 2 - 1) as i:
                body(i)
            scale_weight(pool, FF0, 0, 2, None)
            scale_weight(pool, FF0 + 1, 1, 2, None)
            body(N_OUT // 2 - 1, last=True)

        def s3_tensor(pe):
            rms_sums(pe, [(acc_o[0], ones_half, 12), (acc_o[1], ones_half, 12)], 6)
            for b in range(6):
                rms_spread(pe, G + 1, b, G + b + 1, 7 - b % 2, G + b - 1 if b > 1 else None)

            def body(i, first=False):
                for second in range(2):
                    n = i * 2 + (OUT0 + second)
                    pe.wait_ge(w_lo, n + 1)
                    for g in range(G):
                        c = i * 6 + (3 * second + g)
                        if first and second == 0:
                            pe.wait_ge(oh_lo, KT * (g + 1))
                        at_least(pe, r_free, (c - G) * 2 + 2)
                        project(ps[:, 2 * g, :], second, g, range(KT // 2))
                        mm = project(ps[:, 2 * g + 1, :], second, g, range(KT // 2, KT))
                        mm.then_inc(o_rdy if g < 2 else w_done, 1)

            body(0, True)
            with pe.Fori(1, N_OUT // 2) as i:
                body(i)

        def s3_scalar(act):
            rms_std(act, G + 1, 24, 6)
            split_hi(act, OUT0, 0, OUT0 + 1)

            def split(g):
                for k in range(KT):
                    nc.scalar.activation(NH[:, k, cols(g)], H[:, k, cols(g)], ACT.Copy).then_inc(oh_hi, 1)

            split(0)
            for b in range(6):
                half, g = divmod(b, 3)
                rms_row(act, G + b + 1, 7 - b % 2, acc_o[half][:, cols(g)])
            split(1)
            split(2)

            def body(i):
                for second in range(2):
                    n = i * 2 + (OUT0 + second)
                    split_hi(act, n + 1, 1 - second, n + 2)
                    for g in range(G):
                        c = i * 6 + (3 * second + g)
                        act.wait_ge(h_up, c + 1)
                        at_least(act, h_acc, c)
                        src = H[:, bass.ds(i * 2 + second, 1), cols(g)].rearrange("p a n -> p (a n)")
                        nc.scalar.activation(sqh[:, (3 * second + g) % 2, :], src, ACT.Square).then_inc(h_sq, 1)

            body(0)
            with act.Fori(1, N_OUT // 2) as i:
                body(i)

        def s3_vector(dve):
            rms_recip(dve, G + 1, 24)
            split_lo(dve, OUT0, 0)
            for g in range(G):
                for k in range(KT):
                    dve.wait_ge(oh_hi, KT * g + k + 1)
                    nc.vector.tensor_tensor(NL[:, k, cols(g)], H[:, k, cols(g)], NH[:, k, cols(g)].bitcast(F32),
                                            ALU.subtract).then_inc(oh_lo, 1)
            dve.wait_ge(st_ok, G + 6)

            def body(i, first=False):
                for second in range(2):
                    n = i * 2 + (OUT0 + second)
                    split_lo(dve, n + 1, 1 - second)
                    for g in range(G):
                        c = i * 6 + (3 * second + g)
                        if g < 2:
                            dve.wait_ge(o_rdy, i * 4 + (2 * second + g + 1))
                        else:
                            dve.wait_ge(w_done, n + 1)
                        for half in range(2):
                            nc.vector.tensor_tensor(to[:, g % 2, half, :], ps[:, 2 * g + half, :],
                                                    acc_o[half][:, cols(g)], ALU.mult).then_inc(r_free, 1)
                        dve.wait_ge(r_free, c * 2 + 2)
                        nc.vector.tensor_tensor(to[:, g % 2, 0, :], to[:, g % 2, 0, :], to[:, g % 2, 1, :],
                                                ALU.add).then_inc(r_t, 1)
                        if first and g == 0:
                            dve.wait_ge(x_ld[second], 16 * (G + 1))
                        elif g == 0:
                            pass
                        dve.wait_ge(r_t, c + 1)
                        h = H[:, bass.ds(i * 2 + second, 1), cols(g)].rearrange("p a n -> p (a n)")
                        nc.vector.tensor_tensor(h, h, to[:, g % 2, 0, :], ALU.add).then_inc(h_up, 1)

            body(0, True)
            for k in range(2, KT):
                dve.wait_ge(x_ld[k], 16 * (G + 1))
            with dve.Fori(1, N_OUT // 2) as i:
                body(i)

        n_hi, n_lo, u_done, c_ok, tap, gl_ok, mul_ok, m_hi, m_lo, d_rdy, h_add, f_sq, f_acc, f_hi, f_lo, acc_zero2 = (
            sem(x) for x in ("n_hi", "n_lo", "u_done", "c_ok", "tap", "gl_ok", "mul_ok", "m_hi", "m_lo", "d_rdy", "h_add",
                             "f_sq", "f_acc", "f_hi", "f_lo", "acc_zero2"))
        H_FREE = 2
        CALL4, ROW4 = G + 2, G + 6
        NTILE = KT * G

        def first_tile(j):
            return j * 3 + (FF0 - 1)

        def in_pairs(eng, body):
            with eng.Fori(0, (NJ - 2) // 2) as q:
                body(q * 2 + 1, 0)
                body(q * 2 + 2, 1)
            body(NJ - 1, 0)

        def s4_sync(sp):
            with sp.Fori(0, (N_FF - 2) // 2) as i:
                load_weight(sp, i * 2 + (FF0 + 2), 0)
                load_weight(sp, i * 2 + (FF0 + 3), 1)
            load_weight(sp, PLE0, 0)
            load_weight(sp, PLE0 + 1, 1)
            sp.wait_ge(u_done, 2 * NJ)
            nc.sync.dma_start(rstd_h[:], a["pT"][0:P, :]).then_inc(p_ld, 16)

        def s4_pool(pool):
            pool.sem_inc(h_add, H_FREE)
            pool.sem_inc(mul_ok, 1)

            def body(j, odd):
                n = first_tile(j)
                scale_weight(pool, n, odd, 2, None)
                scale_weight(pool, n + 1, 1 - odd, 2, None)

            in_pairs(pool, body)
            pool.wait_ge(mul_ok, NJ + 1)
            nc.gpsimd.memset(acc_h[:], 0.0).then_inc(acc_zero2, 1)
            pool.wait_ge(acc_zero2, 1)
            for c in range(NTILE):
                g = c % G
                pool.wait_ge(f_sq, c + 1)
                at_least(pool, f_acc, c)
                nc.gpsimd.tensor_tensor(acc_h[:, cols(g)], acc_h[:, cols(g)], sqd[:, c % 2, :], ALU.add).then_inc(f_acc, 1)

        def s4_tensor(pe):
            rms_sums(pe, [(rstd_h, ones_d, 12)], 6)
            for b in range(G):
                rms_spread(pe, CALL4, b, ROW4 + b + 1, 7 - b % 2, ROW4 + 1 if b == 2 else None)

            def up(n, slot, bank, freed, first=False):
                pe.wait_ge(w_lo, n + 1)
                at_least(pe, u_done, freed)
                for g in range(G):
                    if first:
                        pe.wait_ge(n_lo, KT * (g + 1))
                    mm = project(ps[:, bank + g, :], slot, g)
                mm.then_inc(w_done, 1)

            def down(n, slot, j):
                pe.wait_ge(w_lo, n + 1)
                pe.wait_ge(m_lo, j + 1)
                for c in range(NTILE):
                    m, g = divmod(c, G)
                    at_least(pe, h_add, j * NTILE + (c - 2 + 1 + H_FREE))
                    mm = three_pass(ps[:, 6 + c % 2, :], WH[:, slot, cols(m, P)], WL[:, slot, cols(m, P)], MH[:, cols(g)],
                                    ML[:, cols(g)], True, True)
                    mm.then_inc(d_rdy if c < NTILE - 1 else w_done, 1)

            up(FF0, 0, 0, 0, True)
            up(FF0 + 1, 1, 3, 0)
            pe.wait_ge(st_ok, ROW4 + G)

            def body(j, odd):
                n = first_tile(j)
                up(n, odd, 0, j * 2 - 1)
                up(n + 1, 1 - odd, 3, j * 2)
                down(n + 2, odd, j - 1)

            in_pairs(pe, body)
            down(PLE0 - 1, 1, NJ - 1)

        def s4_scalar(act):
            rms_std(act, CALL4, 12, 6)
            for g in range(G):
                for k in range(KT):
                    nc.scalar.activation(NH[:, k, cols(g)], H[:, k, cols(g)], ACT.Copy).then_inc(n_hi, 1)
                if g == 0:
                    for b in range(G):
                        rms_row(act, ROW4 + b + 1, 7 - b % 2, rstd_h[:, cols(b)])

            def centre(j, gate):
                act.wait_ge(u_done, j * 2 + 1 + gate)
                f = j + NJ * gate
                if gate:
                    act.wait_ge(mul_ok, j + 1)
                else:
                    at_least(act, m_lo, j)
                nc.scalar.activation((cg if gate else ca)[:], u[:], ACT.Identity, bias=convb[:, bass.ds(f, 1)],
                                     scale=convw[:, bass.ds(f, 1), 1:2].rearrange("p a b -> p (a b)")).then_inc(c_ok, 1)

            def gate_out(j):
                centre(j, 1)
                act.wait_ge(tap, j * 8 + 8)
                nc.scalar.activation(cg[:], cg[:], ACT.Gelu_apprx_tanh).then_inc(gl_ok, 1)
                act.wait_ge(mul_ok, j + 2)
                if isinstance(j, int) and j == NJ - 1:
                    act.wait_ge(w_done, PLE0 - 1)
                else:
                    act.wait_ge(w_done, first_tile(j + 1))
                nc.scalar.activation(MH[:], ca[:], ACT.Copy).then_inc(m_hi, 1)

            split_hi(act, FF0 + 1, 1, FF0 + 2)
            split_hi(act, FF0 + 2, 0, FF0 + 3)
            centre(0, 0)

            def body(j, odd, last=False):
                n = first_tile(j)
                scaled = FF0 + 1 + j * 2
                split_hi(act, n + 1, 1 - odd, scaled + 1)
                gate_out(j - 1)
                split_hi(act, n + 2, odd, None)
                centre(j, 0)
                split_hi(act, n + 3, 1 - odd, None if last else scaled + 2)

            with act.Fori(0, (NJ - 2) // 2) as q:
                body(q * 2 + 1, 0)
                body(q * 2 + 2, 1)
            body(NJ - 1, 0, True)
            split_hi(act, PLE0, 0, None)
            gate_out(NJ - 1)
            act.wait_ge(m_lo, NJ)
            for c in range(NTILE):
                m, g = divmod(c, G)
                act.wait_ge(h_add, (NJ - 1) * NTILE + c + 1 + H_FREE)
                nc.scalar.activation(NH[:, m, cols(g)], H[:, m, cols(g)], ACT.Copy).then_inc(f_hi, 1)
                at_least(act, f_acc, c - 1)
                nc.scalar.activation(sqd[:, c % 2, :], H[:, m, cols(g)], ACT.Square).then_inc(f_sq, 1)

        def s4_vector(dve):
            rms_recip(dve, CALL4, 12)
            for g in range(G):
                for k in range(KT):
                    dve.wait_ge(n_hi, KT * g + k + 1)
                    nc.vector.tensor_tensor(NL[:, k, cols(g)], H[:, k, cols(g)], NH[:, k, cols(g)].bitcast(F32),
                                            ALU.subtract).then_inc(n_lo, 1)

            def taps(j, gate, n):
                dve.wait_ge(w_done, n + 1)
                at_least(dve, tap, j * 8 + 4 * gate)
                nc.vector.tensor_tensor(u[:], flat(ps[:, 3 * gate:3 * gate + 3, :]), rstd_h[:], ALU.mult).then_inc(u_done, 1)
                dve.wait_ge(c_ok, j * 2 + 1 + gate)
                f = j + NJ * gate
                buf = cg if gate else ca
                t0 = j * 8 + 4 * gate
                for x, (w, to_, from_) in enumerate((
                        (0, slice(1, TP), slice(0, TP - 1)), (0, slice(TP + 1, T), slice(TP, T - 1)),
                        (2, slice(0, TP - 1), slice(1, TP)), (2, slice(TP, T - 1), slice(TP + 1, T)))):
                    if x > 1:
                        dve.wait_ge(tap, t0 + x - 1)
                    nc.vector.scalar_tensor_tensor(buf[:, to_], u[:, from_], convw[:, bass.ds(f, 1), w:w + 1].rearrange("p a b -> p (a b)"),
                                                   buf[:, to_], ALU.mult, ALU.add).then_inc(tap, 1)

            def gate_out(j, n):
                taps(j, 1, n)
                dve.wait_ge(gl_ok, j + 1)
                nc.vector.tensor_tensor(ca[:], ca[:], cg[:], ALU.mult).then_inc(mul_ok, 1)
                dve.wait_ge(m_hi, j + 1)
                nc.vector.tensor_tensor(ML[:], ca[:], MH[:].bitcast(F32), ALU.subtract).then_inc(m_lo, 1)

            def add_down(j, n, extra=False):
                for c in range(NTILE):
                    m, g = divmod(c, G)
                    if c < NTILE - 1:
                        dve.wait_ge(d_rdy, j * (NTILE - 1) + (c + 1))
                    else:
                        dve.wait_ge(w_done, n + 1)
                    h = H[:, m, cols(g)]
                    nc.vector.tensor_tensor(h, h, ps[:, 6 + c % 2, :], ALU.add).then_inc(h_add, 1)
                    if extra and c:
                        rest(c - 1)
                if extra:
                    rest(NTILE - 1)

            def rest(c):
                m, g = divmod(c, G)
                dve.wait_ge(f_hi, c + 1)
                nc.vector.tensor_tensor(NL[:, m, cols(g)], H[:, m, cols(g)], NH[:, m, cols(g)].bitcast(F32),
                                        ALU.subtract).then_inc(f_lo, 1)

            dve.wait_ge(st_ok, ROW4 + G)
            split_lo(dve, FF0 + 1, 1)
            split_lo(dve, FF0 + 2, 0)
            taps(0, 0, FF0)

            def body(j, odd):
                n = first_tile(j)
                split_lo(dve, n + 1, 1 - odd)
                if isinstance(j, int) and j == 1:
                    gate_out(0, FF0 + 1)
                else:
                    gate_out(j - 1, n - 2 if not isinstance(j, int) or j > 1 else FF0 + 1)
                split_lo(dve, n + 2, odd)
                taps(j, 0, n)
                split_lo(dve, n + 3, 1 - odd)
                add_down(j - 1, n + 2)

            in_pairs(dve, body)
            split_lo(dve, PLE0, 0)
            gate_out(NJ - 1, first_tile(NJ - 1) + 1)
            add_down(NJ - 1, PLE0 - 1, True)

        CALL5, ROW5 = CALL4 + 1, ROW4 + G
        CALL6, ROW6 = CALL5 + 1, ROW5 + G
        acc_zero3, pl_rdy, gt_rdy, g_t, g_sig, g_mul, g_up, g_sq, g_acc, y_ok = (
            sem(x) for x in ("acc_zero3", "pl_rdy", "gt_rdy", "g_t", "g_sig", "g_mul", "g_up", "g_sq", "g_acc", "y_ok"))
        UP_FREE, ACC_FREE = 6, 2
        NQ = KT // 2
        SCALED4 = FF0 + 2 * NJ

        def in_halves(eng, body):
            with eng.Fori(0, NQ // 2) as r:
                body(r * 2, 0)
                body(r * 2 + 1, 1)

        def s5_sync(sp):
            sp.wait_ge(p_lo, 1)
            nc.sync.dma_start(rstd_h[:], a["pT"][P:2 * P, :]).then_inc(p_ld, 16)
            with sp.Fori(0, (N_PLE - 2) // 2) as i:
                load_weight(sp, i * 2 + (PLE0 + 2), 0)
                load_weight(sp, i * 2 + (PLE0 + 3), 1)
            load_weight(sp, NW, 0)
            for k in range(KT):
                sp.wait_ge(y_ok, k + 1)
                nc.sync.dma_start(a["yT"][cols(k, P), :], H[:, k, :]).then_inc(stored, 16)
            sp.wait_ge(stored, 16 * KT)
            sp.wait_ge(w_ld[0], landed(NW, 0))

        def s5_pool(pool):
            pool.sem_inc(g_up, UP_FREE)
            pool.sem_inc(g_acc, ACC_FREE)
            pool.wait_ge(st_mm, CALL5)
            nc.gpsimd.memset(acc_h[:], 0.0).then_inc(acc_zero3, 1)

            def body(q, odd):
                n = q * 3 + PLE0
                scale_weight(pool, n + 1, 1 - odd, 3, None)
                scale_weight(pool, n + 2, odd, 3, None)

            in_halves(pool, body)

        def s5_tensor(pe):
            rms_sums(pe, [(acc_h, ones_d, 12)], 6)
            for b in range(G):
                rms_spread(pe, CALL5, b, ROW5 + b + 1, 7 - b % 2, ROW5 + 1 if b == 2 else None)
            pe.wait_ge(p_lo, 2)
            pe.wait_ge(st_ok, ROW5 + G)

            def body(q, odd):
                n = q * 3 + PLE0
                pe.wait_ge(w_lo, n + 1)
                for c in range(6):
                    mm_, g = divmod(c, G)
                    pe.wait_ge(g_up, q * 6 + (c + 1))
                    for k in range(2):
                        w = cols(2 * mm_ + k, P)
                        mm = three_pass(ps[:, c, :], WH[:, odd, w], WL[:, odd, w], PH[:, k, cols(g)], PL[:, k, cols(g)],
                                        k == 0, k == 1)
                    mm.then_inc(pl_rdy if c < 5 else w_done, 1)
                for second in range(2):
                    slot = (odd + 1 + second) % 2
                    pe.wait_ge(w_lo, n + 2 + second)
                    for g in range(G):
                        c = 3 * second + g
                        pe.wait_ge(g_acc, q * 6 + (c - 2 + 1 + ACC_FREE))
                        mm = project(ps[:, 6 + c % 2, :], slot, g)
                        mm.then_inc(gt_rdy if g < 2 else w_done, 1)

            in_halves(pe, body)
            pe.wait_ge(g_acc, NQ * 6 + ACC_FREE)
            rms_sums(pe, [(acc_h, ones_d, 12)], 0)
            for b in range(G):
                rms_spread(pe, CALL6, b, ROW6 + b + 1, 1 + b)

        def s5_scalar(act):
            act.wait_ge(p_ld, 16)
            nc.scalar.activation(PH[:, 0, :], rstd_h[:], ACT.Copy).then_inc(p_hi, 1)
            rms_std(act, CALL5, 12, 6)
            act.wait_ge(p_ld, 32)
            nc.scalar.activation(PH[:, 1, :], rstd_h[:], ACT.Copy).then_inc(p_hi, 1)
            act.wait_ge(p_lo, 2)
            for b in range(G):
                rms_row(act, ROW5 + b + 1, 7 - b % 2, rstd_h[:, cols(b)])

            def body(q, odd):
                n = q * 3 + PLE0
                split_hi(act, n + 1, 1 - odd, q * 2 + (SCALED4 + 1))
                for second in range(2):
                    slot = (odd + second) % 2
                    split_hi(act, n + 2 + second, slot, q * 2 + (SCALED4 + 2) if second == 0 else None)
                    for g in range(G):
                        c = 3 * second + g
                        act.wait_ge(g_t, q * 6 + (c + 1))
                        nc.scalar.activation(gate_t[:], gate_t[:], ACT.Sigmoid).then_inc(g_sig, 1)
                        act.wait_ge(g_up, q * 6 + (c + 1 + UP_FREE))
                        src = H[:, bass.ds(q * 2 + second, 1), cols(g)].rearrange("p a n -> p (a n)")
                        nc.scalar.activation(ps[:, 6 + c % 2, :], src, ACT.Square).then_inc(g_sq, 1)

            in_halves(act, body)
            rms_std(act, CALL6, 12, 0)
            for b in range(G):
                rms_row(act, ROW6 + b + 1, 1 + b, rstd_h[:, cols(b)])

        def s5_vector(dve):
            def p_low(k):
                dve.wait_ge(p_hi, k + 1)
                nc.vector.tensor_tensor(PL[:, k, :], rstd_h[:], PH[:, k, :].bitcast(F32), ALU.subtract).then_inc(p_lo, 1)

            p_low(0)
            rms_recip(dve, CALL5, 12)
            p_low(1)
            dve.wait_ge(st_ok, ROW5 + G)
            dve.wait_ge(acc_zero3, 1)

            def body(q, odd):
                n = q * 3 + PLE0
                split_lo(dve, n + 1, 1 - odd)
                for second in range(2):
                    split_lo(dve, n + 2 + second, (odd + second) % 2)
                    for g in range(G):
                        c = 3 * second + g
                        if g < 2:
                            dve.wait_ge(gt_rdy, q * 4 + (2 * second + g + 1))
                        else:
                            dve.wait_ge(w_done, n + 2 + second)
                        bank = ps[:, 6 + c % 2, :]
                        nc.vector.tensor_tensor(gate_t[:], bank, rstd_h[:, cols(g)], ALU.mult).then_inc(g_t, 1)
                        dve.wait_ge(g_sig, q * 6 + (c + 1))
                        if c < 3:
                            dve.wait_ge(w_done, n + 1)
                        nc.vector.tensor_tensor(gate_t[:], gate_t[:], ps[:, c, :], ALU.mult).then_inc(g_mul, 1)
                        dve.wait_ge(g_mul, q * 6 + (c + 1))
                        h = H[:, bass.ds(q * 2 + second, 1), cols(g)].rearrange("p a n -> p (a n)")
                        nc.vector.tensor_tensor(h, h, gate_t[:], ALU.add).then_inc(g_up, 1)
                        dve.wait_ge(g_sq, q * 6 + (c + 1))
                        nc.vector.tensor_tensor(acc_h[:, cols(g)], acc_h[:, cols(g)], bank, ALU.add).then_inc(g_acc, 1)

            in_halves(dve, body)
            rms_recip(dve, CALL6, 12)
            dve.wait_ge(st_ok, ROW6 + G)
            for k in range(KT):
                nc.vector.scalar_tensor_tensor(H[:, k, :], H[:, k, :], final_g[:, k:k + 1], rstd_h[:], ALU.mult,
                                               ALU.mult).then_inc(y_ok, 1)

        p_ld, p_hi, p_lo = sem("p_ld"), sem("p_hi"), sem("p_lo")
        block = ctx.enter_context(nc.Block())

        @block.sync
        def _(sp):
            s1_sync(sp)
            end_stage(sp, 0)
            s2_sync(sp)
            end_stage(sp, 1)
            s3_sync(sp)
            end_stage(sp, 2)
            s4_sync(sp)
            end_stage(sp, 3)
            s5_sync(sp)

        @block.gpsimd
        def _(pool):
            s1_pool(pool)
            end_stage(pool, 0)
            s2_pool(pool)
            end_stage(pool, 1)
            s3_pool(pool)
            end_stage(pool, 2)
            s4_pool(pool)
            end_stage(pool, 3)
            s5_pool(pool)

        @block.tensor
        def _(pe):
            s1_tensor(pe)
            end_stage(pe, 0)
            s2_tensor(pe)
            end_stage(pe, 1)
            s3_tensor(pe)
            end_stage(pe, 2)
            s4_tensor(pe)
            end_stage(pe, 3)
            s5_tensor(pe)

        @block.scalar
        def _(act):
            s1_scalar(act)
            end_stage(act, 0)
            s2_scalar(act)
            end_stage(act, 1)
            s3_scalar(act)
            end_stage(act, 2)
            s4_scalar(act)
            end_stage(act, 3)
            s5_scalar(act)

        @block.vector
        def _(dve):
            s1_vector(dve)
            end_stage(dve, 0)
            s2_vector(dve)
            end_stage(dve, 1)
            s3_vector(dve)
            end_stage(dve, 2)
            s4_vector(dve)
            end_stage(dve, 3)
            s5_vector(dve)


def shape_constants():
    f = np.float32
    k = np.arange(P)
    out = {"ident": np.eye(P, dtype=f), "ones_d": np.full((P, 1), 1.0 / D, f),
           "ones_half": np.full((P, 1), 2.0 / D, f), "eps": np.full((P, 1), EPS, f),
           "blk": np.where(k[:, None] // DH == k[None, :] // DH, f(1.0 / DH), f(0)).astype(f)}
    perm = np.zeros((P, P), f)
    first = k[k % 32 < 16]
    perm[first + 16, first] = -1.0
    perm[first, first + 16] = 1.0
    out["perm"] = perm
    t = np.arange(TS)
    freqs = (10000.0 ** (-np.arange(0, DH // 2, 2, dtype=f) / f(DH // 2))).astype(f)
    pos = np.where((k[:, None] % DH) < DH // 2, (t // GRID)[None, :], (t % GRID)[None, :]).astype(f)
    ang = pos * freqs[k % 16][:, None]
    out["rope_c"], out["rope_s"] = np.cos(ang).astype(f), np.sin(ang).astype(f)
    c = k[:, None] % GRID
    start = np.clip(c - NA_KW // 2, 0, GRID - NA_KW)
    kc = np.arange(GRID)[None, :]
    out["colmask"] = np.where((kc >= start) & (kc < start + NA_KW), f(0), f(NEG)).astype(f)
    return out


def layout(x):
    def cat_t(p, s):
        return np.concatenate([p.reshape(-1, p.shape[-1]), s.reshape(-1, s.shape[-1])], 0).T

    def feature_rows(v):
        return v.reshape(-1, P).T

    def tile(w, columns):
        return w[:, columns].reshape(-1, P, P).transpose(1, 0, 2).reshape(P, -1)

    w_in, w_out, w_up = x["w_in"][0], x["w_out"][0], x["w_up"][0]
    w_down, w_gate, w_ple = x["w_down"][0], x["w_ple_gate"][0], x["w_ple"][0]
    pair = np.concatenate([np.concatenate([np.arange(DH) + DH * i, np.arange(DH) + DH * (i + 4)]) for i in range(4)])
    k = np.arange(P)
    head = [pair[:P], pair[P:2 * P], pair[2 * P:3 * P], pair[3 * P:], 512 + k]
    plain = [640 + k] + [768 + 512 * part + P * i + k for i in range(4) for part in range(3)]
    order = [y for two in zip(head, plain[:NA_TILES]) for y in two] + plain[NA_TILES:]
    rows = np.concatenate([pair, 512 + np.arange(512)])
    tiles = [tile(w_in, q) for q in order]
    tiles += [tile(w_out[rows], P * m + k) for m in range(KT)]

    def up(j, gate):
        return tile(w_up, FF * gate + P * j + k)

    tiles += [up(0, 0), up(0, 1)]
    for j in range(1, NJ):
        tiles += [up(j, 0), up(j, 1), w_down[P * (j - 1):P * j]]
    tiles.append(w_down[P * (NJ - 1):])
    for q in range(4):
        both = np.concatenate([tile(w_ple, P * (2 * q + m) + k) for m in range(2)], 1)
        tiles += [np.pad(both, ((0, 0), (0, D - both.shape[1]))), tile(w_gate, P * 2 * q + k), tile(w_gate, P * (2 * q + 1) + k)]
    tiles.append(np.zeros((P, D), np.float32))
    conv = x["conv_w"][0].reshape(3, 2 * NJ, P).transpose(2, 1, 0).reshape(P, -1)
    o_gain = np.concatenate([x["out_norm_a"][0][pair], x["out_norm_b"][0]])
    gains = np.concatenate([feature_rows(x["attn_norm"][0]), feature_rows(o_gain), feature_rows(x["ffn_norm"][0]),
                            feature_rows(x["ple_norm"][0])], 1)
    qg = np.concatenate([x["q_norm_a"][0]] * 2)[:, None]
    kg = np.concatenate([x["k_norm_a"][0]] * 2)[:, None]
    arrays = {"w": np.stack(tiles), "xT": cat_t(x["x_prompt"], x["x_sample"]), "pT": cat_t(x["p_prompt"][0], x["p_sample"][0]),
              "gains": gains, "final_g": feature_rows(x["final_norm"]), "qk_g": np.concatenate([qg] * 4 + [kg], 1),
              "convw": conv, "convb": feature_rows(x["conv_b"][0]), "rpb": np.pad(x["rpb_b"][0][:, :, ::-1].reshape(-1), RPB_PAD)[None, :]}
    arrays.update(shape_constants())
    return {n: np.ascontiguousarray(v) for n, v in arrays.items()}


def program(nc, arrays):
    a = {}
    for name, v in arrays.items():
        h = nc.dram_tensor(f"in_{name}", v.shape, mybir.dt.from_np(v.dtype), kind="ExternalInput")
        a[name] = h.ap()
        if name == "rpb":
            a["rpb_tensor"] = h
    a["qkv"] = nc.dram_tensor("qkv", (N_IN, P, T), F32, kind="Internal").ap()
    a["yT"] = nc.dram_tensor("out_yT", (D, T), F32, kind="ExternalOutput").ap()
    build(nc, a)


def kernel(**inputs):
    import concourse.bacc as bacc
    from concourse.bass_utils import run_bass_kernel_spmd

    arrays = layout({n: np.asarray(v) for n, v in inputs.items()})
    nc = bacc.Bacc("TRN2", target_bir_lowering=False, num_devices=1)
    program(nc, arrays)
    r = run_bass_kernel_spmd(nc, [{f"in_{n}": v for n, v in arrays.items()}], core_ids=[0])
    y = r.results[0]["out_yT"]
    return (np.ascontiguousarray(y[:, :TP].T)[None], np.ascontiguousarray(y[:, TP:].T)[None])
```

```python
from contextlib import ExitStack

import numpy as np

import concourse.bass as bass
from concourse import mybir

F32 = mybir.dt.float32
F32R = mybir.dt.float32r
ALU = mybir.AluOpType
ACT = mybir.ActivationFunctionType
AXX = mybir.AxisListType.X

P = 128
D = 1024
KT = D // P
TP, TS = 512, 1024
T = TP + TS
GT = 512
G = T // GT
DH = 64
NPAIR_A, NPAIR_B = 4, 4
NPAIR = NPAIR_A + NPAIR_B
FF = 2816
NJ = FF // P
PLE = 256
EPS = 1e-6
GRID = 64
NA_KH, NA_KW = 8, 16
RPB_R, RPB_C = 2 * NA_KH - 1, 2 * NA_KW - 1
RPB_PAD = GRID - NA_KW
NEG = 1e30
QSCALE = 1.0 / np.sqrt(DH)

N_IN = 18
N_OUT = 8
N_FF = 3 * NJ
N_PLE = 12
OUT0 = N_IN
FF0 = OUT0 + N_OUT
PLE0 = FF0 + N_FF
NW = PLE0 + N_PLE
NA_TILES = 5

ITEMS = 24


def item(m):
    s, n = divmod(m, 12)
    g, t = divmod(n, 4)
    return s, g, t, 3 * s + g


def window(kind, m):
    _, g, t, _ = item(m)
    if kind == "A":
        return (0, TP, None, 0) if g == 0 else (TP, TS, None, 0)
    rows = (TP if g == 0 else TS) // GRID
    r = 2 * (t if g == 0 else 4 * (g - 1) + t)
    first = min(max(r - NA_KH // 2, 0), rows - NA_KH)
    base = 0 if g == 0 else TP
    last = min(max(r + 1 - NA_KH // 2, 0), rows - NA_KH)
    if last > first:
        return base + first * GRID, (NA_KH + 1) * GRID, "mid", 0
    return base + first * GRID, NA_KH * GRID, "edge", first - r + NA_KH - 2


def key_blocks(width):
    return [(k, min(P, width - P * k)) for k in range(-(-width // P))]


V1_AT = 6
V0_AT = ITEMS - 1
FILLS = {("V", 0): 0, ("V", 1): V1_AT + 2}
for _m in range(ITEMS):
    FILLS["T", _m] = _m + 1 + (_m > V1_AT)
NFILL = len(FILLS)


def build(nc, a):
    ctx = ExitStack()
    with ctx:
        def sem(name):
            return ctx.enter_context(nc.semaphore(name))

        base = ((nc.sbuf_base + 31) // 32) * 32
        KB = 1024

        class Region:

            def __init__(self, at):
                self.at = at

            def __call__(self, name, shape, dt=F32):
                h = nc.alloc_sbuf_tensor_at(name, [P] + list(shape), dt, offset=self.at)
                self.at += ((int(np.prod(shape)) * 4 + 31) // 32) * 32
                return h

        c = Region(base)
        misc = c("misc", [3 + NA_TILES])
        ones_d, ones_half, eps, qk_g = misc[:, 0:1], misc[:, 1:2], misc[:, 2:3], misc[:, 3:3 + NA_TILES]
        gains = c("gains", [4, KT])
        final_g = c("final_g", [KT])
        convw = c("convw", [2 * NJ, 3])
        convb = c("convb", [2 * NJ])
        tok_std = c("tok_std", [24])
        tok_r = c("tok_r", [24])
        rsum = c("rsum", [ITEMS])
        nmax = c("nmax", [ITEMS])
        rinv = c("rinv", [2, 4])
        ident = c("ident", [P])
        squares0 = c.at
        blk = c("blk", [P])
        perm = c("perm", [P])
        colmask = c("colmask", [GRID])
        gate_t = nc.alloc_sbuf_tensor_at("gate_t", [P, GT], F32, offset=squares0)
        assert c.at <= squares0 + 2 * KB, (c.at, squares0)
        B0 = squares0 + 2 * KB

        c = Region(B0)
        NH = c("NH", [KT, T], F32R)
        NL = c("NL", [KT, T], F32R)
        WH = c("WH", [2, D], F32R)
        WL = c("WL", [2, D], F32R)
        raw = c("raw", [2, D])
        H0 = c.at
        H = c("H", [KT, T])
        X0 = c.at
        END = nc.sbuf_usable_end

        c = Region(H0)
        xst = c("xst", [KT, GT])
        sqx = c("sqx", [2, GT])
        accx = c("accx", [GT])
        rstd = c("rstd", [T])
        oa = c("oa", [T])
        ob = c("ob", [T])
        rope_c = c("rope_c", [TS])
        rope_s = c("rope_s", [TS])
        qs = c("qs", [G, GT])
        qsq = c("qsq", [2, GT])
        qstd = c("qstd", [2, GT])
        qn = c("qn", [2, GT])
        qt = c("qt", [2, GT])
        assert c.at <= END

        c = Region(B0)
        QS = [c(f"QS{s}", [T], F32R) for s in range(2)]
        KH = [c(f"KH{s}", [T], F32R) for s in range(2)]
        KL = [c(f"KL{s}", [T], F32R) for s in range(2)]
        VT = [c(f"VT{s}", [T // P, P], F32R) for s in range(2)]
        PTH = c("PTH", [2, TS // P, 2 * P], F32R)
        PTL = c("PTL", [2, TS // P, 2 * P], F32R)
        qraw = [c(f"qraw{s}", [T]) for s in range(2)]
        kraw = [c(f"kraw{s}", [T]) for s in range(2)]
        PR = c("PR", [2, TS])
        SC = c("SC", [2, 9 * GRID])
        TR = c("TR", [14, GRID])
        assert c.at <= H0, (c.at, H0)
        c = Region(X0)
        vraw = c("vraw", [T])
        acc_o = [c("acc_a", [T]), c("acc_b", [T])]
        sqo = c("sqo", [GT])
        osum = c("osum", [GT])
        TE = [c(f"TE{s}", [14, GRID]) for s in range(2)]
        TM = [c(f"TM{s}", [9, GRID]) for s in range(2)]
        assert c.at <= END, (c.at, END)

        c = Region(X0)
        rstd_h = c("rstd_h", [T])
        c = Region(X0 + 18 * KB)
        to = c("to", [2, 2, GT])
        sqh = c("sqh", [2, GT])
        assert c.at <= END
        c = Region(X0 + 6 * KB)
        u = c("u", [T])
        ca = c("ca", [T])
        cg = c("cg", [T])
        MH = c("MH", [T], F32R)
        ML = c("ML", [T], F32R)
        assert c.at <= END, (c.at, END)
        c = Region(X0 + 6 * KB)
        acc_h = c("acc_h", [T])
        PH = c("PH", [2, T], F32R)
        PL = c("PL", [2, T], F32R)
        sqd = nc.alloc_sbuf_tensor_at("sqd", [P, 2, GT], F32, offset=X0 + 12 * KB)

        ps = ctx.enter_context(nc.psum_tensor("ps", [P, 8, GT], F32))

        def flat(t):
            return t.rearrange("p a b -> p (a b)")

        def at_least(eng, s, v):
            if not isinstance(v, int) or v > 0:
                eng.wait_ge(s, v)

        def cols(g, n=GT):
            return slice(g * n, (g + 1) * n)

        c_ld = sem("c_ld")
        w_ld = [sem("w_ld0"), sem("w_ld1")]
        w_sc = sem("w_sc")
        w_hi = sem("w_hi")
        w_lo = sem("w_lo")
        w_done = sem("w_done")
        stage_end = [sem(f"stage_end{k}") for k in range(4)]
        stored = sem("stored")

        def end_stage(eng, k):
            eng.drain().then_inc(stage_end[k], 1)
            eng.wait_ge(stage_end[k], 5)

        def load_weight(sp, n, slot, wait=True):
            if wait:
                at_least(sp, w_lo, n - 1)
            src = a["w"][bass.ds(n, 1)].rearrange("a p n -> p (a n)")
            nc.sync.dma_start(raw[:, slot, :], src).then_inc(w_ld[slot], 16)

        def scale_weight(pool, n, slot, which, scaled):
            pool.wait_ge(w_ld[slot], landed(n, slot))
            v = raw[:, slot, :].rearrange("p (k n) -> p k n", k=KT)
            g = gains[:, which, :].unsqueeze(2).to_broadcast([P, KT, P])
            nc.gpsimd.tensor_tensor(v, v, g, ALU.mult).then_inc(w_sc, 1)

        def landed(n, slot):
            if isinstance(n, int):
                return 16 * (n // 2 + 1)
            return (n - slot) * 8 + 16

        def split_hi(act, n, slot, scaled):
            if scaled is None:
                act.wait_ge(w_ld[slot], landed(n, slot))
            else:
                act.wait_ge(w_sc, scaled)
            at_least(act, w_done, n - 1)
            nc.scalar.activation(WH[:, slot, :], raw[:, slot, :], ACT.Copy).then_inc(w_hi, 1)

        def split_lo(dve, n, slot):
            dve.wait_ge(w_hi, n + 1)
            nc.vector.tensor_tensor(WL[:, slot, :], raw[:, slot, :], WH[:, slot, :].bitcast(F32),
                                    ALU.subtract).then_inc(w_lo, 1)

        def three_pass(out, wh, wl, xh, xl, first, last):
            nc.tensor.matmul(out, wh, xh, start=first, stop=False)
            nc.tensor.matmul(out, wh, xl, start=False, stop=False)
            return nc.tensor.matmul(out, wl, xh, start=False, stop=last)

        def project(out, slot, g, ks=range(KT)):
            for k in ks:
                mm = three_pass(out, WH[:, slot, cols(k, P)], WL[:, slot, cols(k, P)],
                                NH[:, k, cols(g)], NL[:, k, cols(g)], k == ks[0], k == ks[-1])
            return mm

        st_mm, st_std, st_r, st_bc, st_ok = (sem(f"st_{x}") for x in ("mm", "std", "r", "bc", "ok"))

        def rms_sums(pe, parts, bank):
            j = 0
            for acc, ones, n in parts:
                for i in range(n):
                    mm = nc.tensor.matmul(ps[:, bank, j:j + 1], acc[:, cols(i, P)], ones[:, 0:1], start=True, stop=True)
                    j += 1
            mm.then_inc(st_mm, 1)

        def rms_std(act, call, n, bank):
            act.wait_ge(st_mm, call)
            nc.scalar.activation(tok_std[:, 0:n], ps[:, bank, 0:n], ACT.Sqrt, bias=eps[:, 0:1]).then_inc(st_std, 1)

        def rms_recip(dve, call, n):
            dve.wait_ge(st_std, call)
            nc.vector.reciprocal(tok_r[:, 0:n], tok_std[:, 0:n]).then_inc(st_r, 1)

        def rms_spread(pe, call, b, number, bank, free=None):
            pe.wait_ge(st_r, call)
            if free is not None:
                pe.wait_ge(st_ok, free)
            for j in range(4):
                col = tok_r[:, 4 * b + j:4 * b + j + 1].to_broadcast([P, P])
                mm = nc.tensor.transpose(ps[:, bank, cols(j, P)], col, ident[:, :])
            mm.then_inc(st_bc, 1)

        def rms_row(act, number, bank, dst):
            act.wait_ge(st_bc, number)
            nc.scalar.activation(dst, ps[:, bank, :], ACT.Copy).then_inc(st_ok, 1)

        x_ld = [sem(f"x_ld{k}") for k in range(KT)]
        x_sq, x_acc, x_hi, x_lo = (sem(f"x_{x}") for x in ("sq", "acc", "hi", "lo"))
        p_rdy = sem("p_rdy")
        a_ev, b_ev = sem("a_ev"), sem("b_ev")
        q_sq, q_mean, q_std, q_rec, q_n, q_rot, q_part, q_fin = (
            sem(f"q_{x}") for x in ("sq", "mean", "std", "rec", "n", "rot", "part", "fin"))
        st_a, st_b = sem("st_a"), sem("st_b")
        BODIES = N_IN // 2

        def group_ready(eng, n, g):
            if g < 2:
                eng.wait_ge(p_rdy, 2 * n + g + 1)
            else:
                eng.wait_ge(w_done, n + 1)

        def signal_group(mm, g):
            mm.then_inc(p_rdy if g < 2 else w_done, 1)

        def s1_sync(sp):
            consts = [(ident, "ident"), (blk, "blk"), (perm, "perm"), (colmask, "colmask"), (ones_d, "ones_d"),
                      (ones_half, "ones_half"), (eps, "eps"), (gains, "gains"), (final_g, "final_g"), (qk_g, "qk_g"),
                      (convw, "convw"), (convb, "convb"), (rope_c, "rope_c"), (rope_s, "rope_s")]

            def load_x(g, k):
                at_least(sp, x_lo, KT * (g - 1) + k + 1)
                nc.sync.dma_start(xst[:, k, :], a["xT"][cols(k, P), cols(g)]).then_inc(x_ld[k], 16)

            for k in range(KT):
                load_x(0, k)
            load_weight(sp, 0, 0, wait=False)
            for t, name in consts:
                v = t[:] if len(t.shape) == 2 else flat(t[:])
                nc.sync.dma_start(v, a[name]).then_inc(c_ld, 16)
            load_weight(sp, 1, 1, wait=False)
            for g in (1, 2):
                for k in range(KT):
                    load_x(g, k)

            def body(i, head):
                load_weight(sp, i * 2 + 2, 0)
                load_weight(sp, i * 2 + 3, 1)
                first = i if head else i * 2
                second = i + NA_TILES if head else i * 2 + 1
                sp.wait_ge(q_fin if head else a_ev, (i + 1) * 3)
                nc.sync.dma_start(a["qkv"][bass.ds(first, 1)].rearrange("a p n -> p (a n)"), oa[:]).then_inc(st_a, 16)
                sp.wait_ge(b_ev, (i + 1) * 3)
                nc.sync.dma_start(a["qkv"][bass.ds(second, 1)].rearrange("a p n -> p (a n)"), ob[:]).then_inc(st_b, 16)

            with sp.Fori(0, NA_TILES) as i:
                body(i, True)
            with sp.Fori(NA_TILES, BODIES - 1) as i:
                body(i, False)
            i = BODIES - 1
            sp.wait_ge(a_ev, 3 * (i + 1))
            nc.sync.dma_start(a["qkv"][2 * i], oa[:]).then_inc(st_a, 16)
            sp.wait_ge(b_ev, 3 * (i + 1))
            nc.sync.dma_start(a["qkv"][2 * i + 1], ob[:]).then_inc(st_b, 16)
            sp.wait_ge(st_a, 16 * BODIES)
            sp.wait_ge(st_b, 16 * BODIES)

        NCONST = 14

        def s1_pool(pool):
            pool.wait_ge(c_ld, 16 * NCONST)
            scale_weight(pool, 0, 0, 0, 1)
            for g in range(G):
                for k in range(1, KT):
                    pool.wait_ge(x_sq, KT * g + k + 1)
                    if k == 1:
                        if g:
                            pool.wait_ge(st_mm, g)
                        ins = nc.gpsimd.tensor_tensor(accx[:], sqx[:, 0, :], sqx[:, 1, :], ALU.add)
                    else:
                        pool.wait_ge(x_acc, (KT - 1) * g + k - 1)
                        ins = nc.gpsimd.tensor_tensor(accx[:], accx[:], sqx[:, k % 2, :], ALU.add)
                    ins.then_inc(x_acc, 1)
                if g == 0:
                    scale_weight(pool, 1, 1, 0, 2)
            with pool.Fori(0, BODIES - 1) as i:
                scale_weight(pool, i * 2 + 2, 0, 0, i * 2 + 3)
                scale_weight(pool, i * 2 + 3, 1, 0, i * 2 + 4)

        def s1_tensor(pe):
            pe.wait_ge(c_ld, 16 * NCONST)

            def sums(g):
                pe.wait_ge(x_acc, (KT - 1) * (g + 1))
                rms_sums(pe, [(accx, ones_d, 4)], 4)

            def spread(g):
                rms_spread(pe, g + 1, 0, g + 1, 5, g if g else None)

            def main(i, g, second):
                n = i * 2 + second
                if g == 0:
                    pe.wait_ge(w_lo, n + 1)
                at_least(pe, b_ev if second else a_ev, (i - 1) * 3 + g + 1)
                signal_group(project(ps[:, 3 * second + g, :], second, g), g)

            def mean(i, g):
                pe.wait_ge(q_sq, i * 3 + g + 1)
                at_least(pe, q_std, i * 3 + g)
                nc.tensor.matmul(ps[:, 6, :], blk[:], qsq[:, g % 2, :], start=True, stop=True).then_inc(q_mean, 1)

            def rot(i, g):
                pe.wait_ge(q_n, i * 3 + g + 1)
                at_least(pe, q_part, (i * 3 + g) * 2)
                nc.tensor.matmul(ps[:, 7, :], perm[:], qn[:, g % 2, :], start=True, stop=True).then_inc(q_rot, 1)

            def body(i, first=False):
                for g in range(G):
                    if first:
                        sums(g)
                        pe.wait_ge(x_lo, KT * (g + 1))
                    main(i, g, 0)
                    if first:
                        spread(g)
                    if g == 1:
                        mean(i, 0)
                mean(i, 1)
                rot(i, 0)
                if first:
                    pe.wait_ge(st_ok, G)
                main(i, 0, 1)
                mean(i, 2)
                rot(i, 1)
                main(i, 1, 1)
                rot(i, 2)
                main(i, 2, 1)

            body(0, True)
            with pe.Fori(1, NA_TILES) as i:
                body(i)
            with pe.Fori(NA_TILES, BODIES) as i:
                for second in range(2):
                    for g in range(G):
                        main(i, g, second)

        def s1_scalar(act):
            act.wait_ge(c_ld, 16 * NCONST)
            split_hi(act, 0, 0, 1)

            def x_split(g):
                for k in range(KT):
                    act.wait_ge(x_ld[k], 16 * (g + 1))
                    at_least(act, x_acc, (KT - 1) * g + k - 2 if k > 2 else (KT - 1) * g + (k == 2))
                    nc.scalar.activation(sqx[:, k % 2, :], xst[:, k, :], ACT.Square).then_inc(x_sq, 1)
                    nc.scalar.activation(NH[:, k, cols(g)], xst[:, k, :], ACT.Copy).then_inc(x_hi, 1)

            def square(i, g):
                act.wait_ge(a_ev, i * 3 + g + 1)
                at_least(act, q_mean, i * 3 + (0, -1, 1)[g])
                nc.scalar.activation(qsq[:, g % 2, :], qs[:, g, :], ACT.Square).then_inc(q_sq, 1)

            def std(i, g):
                act.wait_ge(q_mean, i * 3 + g + 1)
                at_least(act, q_n, i * 3 + (0, -1, 1)[g])
                nc.scalar.activation(qstd[:, g % 2, :], ps[:, 6, :], ACT.Sqrt, bias=eps[:, 0:1]).then_inc(q_std, 1)

            def row(g):
                rms_row(act, g + 1, 5, rstd[:, cols(g)])

            x_split(0)
            split_hi(act, 1, 1, 2)
            rms_std(act, 1, 4, 4)
            x_split(1)
            row(0)
            rms_std(act, 2, 4, 4)
            x_split(2)
            square(0, 0)
            row(1)
            square(0, 1)
            std(0, 0)
            rms_std(act, 3, 4, 4)
            row(2)
            square(0, 2)
            std(0, 1)
            split_hi(act, 2, 0, 3)
            std(0, 2)
            with act.Fori(1, NA_TILES) as i:
                split_hi(act, i * 2 + 1, 1, i * 2 + 2)
                square(i, 0)
                square(i, 1)
                std(i, 0)
                square(i, 2)
                std(i, 1)
                split_hi(act, i * 2 + 2, 0, i * 2 + 3)
                std(i, 2)
            with act.Fori(NA_TILES, BODIES - 1) as i:
                split_hi(act, i * 2 + 1, 1, i * 2 + 2)
                split_hi(act, i * 2 + 2, 0, i * 2 + 3)
            split_hi(act, N_IN - 1, 1, N_IN)

        def s1_vector(dve):
            dve.wait_ge(c_ld, 16 * NCONST)
            split_lo(dve, 0, 0)

            def x_low(g):
                for k in range(KT):
                    dve.wait_ge(x_hi, KT * g + k + 1)
                    nc.vector.tensor_tensor(NL[:, k, cols(g)], xst[:, k, :], NH[:, k, cols(g)].bitcast(F32),
                                            ALU.subtract).then_inc(x_lo, 1)

            def out_a(i, g):
                group_ready(dve, i * 2, g)
                nc.vector.tensor_tensor(qs[:, g, :], ps[:, g, :], rstd[:, cols(g)], ALU.mult).then_inc(a_ev, 1)

            def head_norm(i, g):
                k = i * 3 + g
                dve.wait_ge(q_std, k + 1)
                nc.vector.reciprocal(qstd[:, g % 2, :], qstd[:, g % 2, :]).then_inc(q_rec, 1)
                dve.wait_ge(q_rec, k + 1)
                nc.vector.scalar_tensor_tensor(qn[:, g % 2, :], qs[:, g, :], qk_g[:, bass.ds(i, 1)], qstd[:, g % 2, :],
                                               ALU.mult, ALU.mult).then_inc(q_n, 1)

            def rotary(i, g):
                k = i * 3 + g
                tab = cols(max(g - 1, 0))
                dve.wait_ge(q_n, k + 1)
                at_least(dve, q_fin, k)
                nc.vector.tensor_tensor(qt[:, 0, :], qn[:, g % 2, :], rope_c[:, tab], ALU.mult).then_inc(q_part, 1)
                dve.wait_ge(q_rot, k + 1)
                nc.vector.tensor_tensor(qt[:, 1, :], ps[:, 7, :], rope_s[:, tab], ALU.mult).then_inc(q_part, 1)
                dve.wait_ge(q_part, k * 2 + 2)
                if g == 0:
                    dve.wait_ge(st_a, i * 16)
                nc.vector.tensor_tensor(oa[:, cols(g)], qt[:, 0, :], qt[:, 1, :], ALU.add).then_inc(q_fin, 1)

            def out_plain(i, g, second):
                group_ready(dve, i * 2 + second, g)
                if g == 0:
                    dve.wait_ge(st_b if second else st_a, i * 16)
                dst = ob if second else oa
                nc.vector.tensor_tensor(dst[:, cols(g)], ps[:, 3 * second + g, :], rstd[:, cols(g)],
                                        ALU.mult).then_inc(b_ev if second else a_ev, 1)

            def tail(i):
                head_norm(i, 1)
                rotary(i, 0)
                out_plain(i, 0, 1)
                head_norm(i, 2)
                rotary(i, 1)
                out_plain(i, 1, 1)
                rotary(i, 2)
                out_plain(i, 2, 1)

            x_low(0)
            split_lo(dve, 1, 1)
            rms_recip(dve, 1, 4)
            x_low(1)
            dve.wait_ge(st_ok, 1)
            out_a(0, 0)
            rms_recip(dve, 2, 4)
            x_low(2)
            dve.wait_ge(st_ok, 2)
            out_a(0, 1)
            rms_recip(dve, 3, 4)
            head_norm(0, 0)
            dve.wait_ge(st_ok, 3)
            out_a(0, 2)
            split_lo(dve, 2, 0)
            tail(0)
            with dve.Fori(1, NA_TILES) as i:
                split_lo(dve, i * 2 + 1, 1)
                out_a(i, 0)
                out_a(i, 1)
                head_norm(i, 0)
                out_a(i, 2)
                split_lo(dve, i * 2 + 2, 0)
                tail(i)
            with dve.Fori(NA_TILES, BODIES - 1) as i:
                split_lo(dve, i * 2 + 1, 1)
                for g in range(G):
                    out_plain(i, g, 0)
                split_lo(dve, i * 2 + 2, 0)
                for g in range(G):
                    out_plain(i, g, 1)
            split_lo(dve, N_IN - 1, 1)
            for second in range(2):
                for g in range(G):
                    out_plain(BODIES - 1, g, second)

        q_ld, k_ld, v_ld, t_ld, q_hi, k_hi, q_lo, k_lo, tab = (
            [sem(f"{x}{s}") for s in range(2)] for x in ("q_ld", "k_ld", "v_ld", "t_ld", "q_hi", "k_hi", "q_lo", "k_lo", "tab"))
        zeroed, pe_passed, dve_passed = sem("zeroed"), sem("pe_passed"), sem("dve_passed")
        s_rdy, m_done, e_done = sem("s_rdy"), sem("m_done"), sem("e_done")
        t_rdy, t_hi, t_free = ([sem(f"{x}{b}") for b in range(2)] for x in ("t_rdy", "t_hi", "t_free"))
        ri_ok, r_rdy, pv_done, o_copy, o_sum, o_done, o_sq, o_acc = (
            sem(x) for x in ("ri_ok", "r_rdy", "pv_done", "o_copy", "o_sum", "o_done", "o_sq", "o_acc"))
        O_FREE = T_FREE = ACC_FREE_O = TAB_FREE = 1
        TBANK, PVBANK, RBANK = 4, 6, 7
        QROW = {"A": lambda i: (i, 4, 5), "B": lambda i: (i * 3 + 6, i * 3 + 7, i * 3 + 8)}

        def probs(m, w):
            return PR[:, m % 2, 0:w]

        def score_bank(m, w):
            return flat(ps[:, 2 * (m % 2):2 * (m % 2) + 2, :])[:, 0:w]

        def split_blocks(w):
            b = key_blocks(w)
            h = len(b) // 2
            return [b[:h] + b[2 * h:], b[h:2 * h]]

        def places(w):
            b0, b1 = split_blocks(w)
            return sorted((kb, kn, n) for n, (kb, kn) in enumerate(b0 + b1))

        def fills(p, name):
            return p * NFILL + FILLS[name] + 1

        def turned_dst(t, m, w, b):
            n0 = len(split_blocks(w)[0])
            n = len(split_blocks(w)[b])
            return t[:, (m // 2) % 2, n0 * b:n0 * b + n, cols(m % 2, P)]

        def turned_src(b, n):
            return ps[:, TBANK + b, 0:n * P].rearrange("p (a c) -> p a c", c=P)

        def value_src(b):
            return ps[:, TBANK + b, 0:6 * DH].rearrange("p (a c) -> p a c", c=DH)

        def read_out(kind, p, m, before, middle):
            if m == 1 and before and not middle:
                return p - 1, 5
            if m % 4 == 1 and m >= 5 and not middle:
                return p, (m - 5) // 4
            return None

        def every_pair(eng, step):
            def steps(kind, p, i, ms, before, after):
                for m in ms:
                    step(kind, p, i, m, before, after)

            steps("A", 0, 0, range(2), None, "A")
            for kind, p0, n, then in (("A", 0, NPAIR_A, "B"), ("B", NPAIR_A, NPAIR_B, None)):
                with eng.Fori(0, n - 1) as i:
                    steps(kind, i + p0, i, range(2, ITEMS), kind, kind)
                    steps(kind, i + (p0 + 1), i + 1, range(2), kind, kind)
                steps(kind, p0 + n - 1, n - 1, range(2, ITEMS), kind, then)
                if then:
                    steps(then, p0 + n, 0, range(2), kind, then)
            step("B", NPAIR, None, 0, "B", None)
            step("B", NPAIR, None, 1, "B", None)

        def s2_sync(sp):
            def load(kind, p, i, s, first=False):
                q, k, v = QROW[kind](i)
                rows = cols(s, DH)
                for row, dst, hi, lo, done in ((q, qraw, q_hi, q_lo, q_ld), (k, kraw, k_hi, k_lo, k_ld)):
                    if not first:
                        sp.wait_ge(lo[s], p * (G if lo is q_lo else 1))
                    for half in range(2):
                        src = a["qkv"][bass.ds(row, 1), rows, :].rearrange("a p n -> p (a n)")
                        nc.sync.dma_start(dst[s][cols(half, DH), :], src).then_inc(done[s], 16)
                if not first:
                    sp.wait_ge(t_rdy[1], fills(p - 1, ("V", s)))
                src = a["qkv"][bass.ds(v, 1), rows, :].rearrange("a p n -> p (a n)")
                nc.sync.dma_start(vraw[rows, :], src).then_inc(v_ld[s], 16)
                if kind == "B":
                    sp.wait_ge(tab[1 - s], i * 4 + 2 * s + TAB_FREE)
                    for half in range(2):
                        src = bass.AP(tensor=a["rpb_tensor"], offset=(i * 2 + s) * (RPB_R * RPB_C) + RPB_C * (1 - half),
                                      ap=[[1, GRID], [RPB_C, 14], [1, GRID]])
                        nc.sync.dma_start(TR[cols(half, GRID), :, :], src).then_inc(t_ld[s], 16)

            for s in range(2):
                load("A", 0, 0, s, first=True)
            with sp.Fori(1, NPAIR_A) as i:
                for s in range(2):
                    load("A", i, i, s)
            with sp.Fori(0, NPAIR_B) as i:
                for s in range(2):
                    load("B", i + NPAIR_A, i, s)

        def s2_pool(pool):
            for s, count in ((o_done, O_FREE), (o_acc, ACC_FREE_O), (t_free[0], T_FREE), (t_free[1], T_FREE),
                             (tab[0], TAB_FREE), (tab[1], TAB_FREE)):
                pool.sem_inc(s, count)

            def keys_low(p, s):
                pool.wait_ge(k_hi[s], p * G + G)
                nc.gpsimd.tensor_tensor(KL[s][:], kraw[s][:], KH[s][:].bitcast(F32), ALU.subtract).then_inc(k_lo[s], 1)
                pool.wait_ge(k_lo[s], p + 1)

            keys_low(0, 0)
            for s in range(2):
                for n, (v, value) in enumerate(((TM[s][GRID:P, 0, :], NEG), (TM[s][0:GRID, NA_KH, :], NEG), (acc_o[s][:], 0.0))):
                    at_least(pool, zeroed, 3 * s + n)
                    nc.gpsimd.memset(v, value).then_inc(zeroed, 1)
            pool.wait_ge(zeroed, 6)

            def body(half, p, last=False):
                pool.wait_ge(o_acc, p * 6 + ACC_FREE_O)
                keys_low(p, 1)
                for b in range(6):
                    s, g = divmod(b, 3)
                    if b == 3 and not last:
                        pool.wait_ge(o_acc, p * 6 + b + ACC_FREE_O)
                        keys_low(p + 1, 0)
                    rows = cols(s, DH)
                    pool.wait_ge(o_done, p * 6 + b + 1 + O_FREE)
                    pool.wait_ge(o_acc, p * 6 + b + ACC_FREE_O)
                    src = H[rows, bass.ds(p, 1), cols(g)].rearrange("p a n -> p (a n)")
                    nc.gpsimd.tensor_tensor(sqo[rows, :], src, src, ALU.mult).then_inc(o_sq, 1)
                    pool.wait_ge(o_sq, p * 6 + b + 1)
                    v = acc_o[half][rows, cols(g)]
                    nc.gpsimd.tensor_tensor(v, v, sqo[rows, :], ALU.add).then_inc(o_acc, 1)

            with pool.Fori(0, NPAIR_A) as i:
                body(0, i)
            with pool.Fori(NPAIR_A, NPAIR - 1) as i:
                body(1, i)
            body(1, NPAIR - 1, last=True)

        def s2_tensor(pe):
            def values(p, s):
                pe.wait_ge(v_ld[s], (p + 1) * 16)
                for b in range(2):
                    pe.wait_ge(t_free[b], fills(p, ("V", s)) - 1 + T_FREE)
                    pe.sem_inc(pe_passed, 1)
                    for j in range(6):
                        mm = nc.tensor.transpose(ps[:, TBANK + b, cols(j, DH)], vraw[cols(s, DH), cols(6 * b + j, P)],
                                                 ident[cols(s, DH), cols(s, DH)])
                    mm.then_inc(t_rdy[b], 1)

            def scores(kind, p, m):
                s, g, t, _ = item(m)
                k0, w, _, _ = window(kind, m)
                if m % 12 == 0:
                    pe.wait_ge(q_lo[s], p * G + G)
                    pe.wait_ge(k_lo[s], p + 1)
                q = QS[s][:, g * GT + t * P:g * GT + (t + 1) * P]
                for c0 in range(0, w, GT):
                    n = min(GT, w - c0)
                    out = ps[:, 2 * (m % 2) + c0 // GT, 0:n]
                    nc.tensor.matmul(out, q, KH[s][:, k0 + c0:k0 + c0 + n], start=True, stop=False)
                    mm = nc.tensor.matmul(out, q, KL[s][:, k0 + c0:k0 + c0 + n], start=False, stop=True)
                mm.then_inc(s_rdy, 1)

            def turn(kind, p, m):
                _, w, _, _ = window(kind, m)
                pe.wait_ge(e_done, p * ITEMS + m + 1)
                for b, blocks in enumerate(split_blocks(w)):
                    pe.wait_ge(t_free[b], fills(p, ("T", m)) - 1 + T_FREE)
                    for j, (kb, kn) in enumerate(blocks):
                        src = probs(m, w)[:, kb * P:kb * P + kn]
                        mm = nc.tensor.transpose(ps[0:kn, TBANK + b, cols(j, P)], src, ident[:, :])
                    mm.then_inc(t_rdy[b], 1)

            def norm_row(p, b):
                pe.wait_ge(ri_ok, p * 6 + b + 1)
                pe.wait_ge(o_done, p * 6 + b + O_FREE)
                for t in range(4):
                    mm = nc.tensor.transpose(ps[:, RBANK, cols(t, P)], rinv[:, b % 2, t:t + 1].to_broadcast([P, P]),
                                             ident[:, :])
                mm.then_inc(r_rdy, 1)

            def weigh(kind, p, b, m, queries):
                s = b // 3
                k0, w, _, _ = window(kind, m)
                at = (m % 4) * P
                pe.wait_ge(t_free[0], fills(p, ("T", m + queries // P - 1)) + T_FREE)
                pe.wait_ge(t_free[1], fills(p, ("T", m + queries // P - 1)) + T_FREE)
                pe.wait_ge(o_done, p * 6 + b + O_FREE)
                todo = places(w)
                c0 = (m % 2) * P
                for kb, kn, n in todo:
                    for x in (PTH, PTL):
                        mm = nc.tensor.matmul(ps[:, PVBANK, at:at + queries], VT[s][0:kn, k0 // P + kb, :],
                                              x[0:kn, (m // 2) % 2, n, c0:c0 + queries],
                                              start=(kb == 0 and x is PTH), stop=(kb == todo[-1][0] and x is PTL))
                return mm

            def weigh_step(kind, p, m):
                if kind == "A" and m % 2 == 1:
                    mm = weigh(kind, p, (m - 3) // 4, m - 3, 2 * P)
                    if m % 4 == 1:
                        mm.then_inc(pv_done, 1)
                if kind == "B" and m % 2 == 0:
                    weigh(kind, p, (m - 2) // 4, m - 2, P)
                    mm = weigh(kind, p, (m - 2) // 4, m - 1, P)
                    if m % 4 == 0:
                        mm.then_inc(pv_done, 1)

            def step(kind, p, i, m, before, after):
                if i is not None:
                    if m + 2 < ITEMS:
                        pe.wait_ge(e_done if kind == "A" else m_done, p * ITEMS + m + 1)
                        scores(kind, p, m + 2)
                    elif after:
                        pe.wait_ge(e_done if kind == "A" else m_done, p * ITEMS + m + 1)
                        scores(after, p + 1, m + 2 - ITEMS)
                    turn(kind, p, m)
                if m >= 3 or kind == "B" and m == 2:
                    weigh_step(kind, p, m)
                elif m < 2 and before:
                    weigh_step(before, p - 1, m + ITEMS)
                if i is not None and m % 4 == 3:
                    norm_row(p, m // 4)
                if m == V1_AT:
                    values(p, 1)
                if m == V0_AT and after:
                    values(p + 1, 0)

            values(0, 0)
            scores("A", 0, 0)
            scores("A", 0, 1)
            every_pair(pe, step)

        def s2_scalar(act):
            def queries(p, s, g):
                act.wait_ge(q_ld[s], (p + 1) * 32)
                at_least(act, s_rdy, p * ITEMS + 1 if s else p * ITEMS - 12)
                nc.scalar.activation(QS[s][:, cols(g)], qraw[s][:, cols(g)], ACT.Copy, scale=-QSCALE).then_inc(q_hi[s], 1)

            def keys(p, s, g):
                act.wait_ge(k_ld[s], (p + 1) * 32)
                at_least(act, s_rdy, p * ITEMS + 1 if s else p * ITEMS - 12)
                nc.scalar.activation(KH[s][:, cols(g)], kraw[s][:, cols(g)], ACT.Copy).then_inc(k_hi[s], 1)

            def values(p, s):
                for b in range(2):
                    act.wait_ge(t_rdy[b], fills(p, ("V", s)))
                    nc.scalar.activation(VT[s][:, 6 * b:6 * b + 6, 0:DH], value_src(b), ACT.Copy).then_inc(t_hi[b], 1)

            def exps(kind, p, m):
                _, w, _, _ = window(kind, m)
                act.wait_ge(m_done, p * ITEMS + m + 1)
                src = score_bank(m, w) if kind == "A" else SC[:, m % 2, 0:w]
                nc.scalar.activation(probs(m, w), src, ACT.Exp, bias=nmax[:, m:m + 1], scale=-1.0,
                                     accum_out=rsum[:, m:m + 1]).then_inc(e_done, 1)

            def turned(kind, p, m, b):
                _, w, _, _ = window(kind, m)
                act.wait_ge(t_rdy[b], fills(p, ("T", m)))
                nc.scalar.activation(turned_dst(PTH, m, w, b), turned_src(b, len(split_blocks(w)[b])),
                                     ACT.Copy).then_inc(t_hi[b], 1)

            def out_copy(p, b):
                s, g = divmod(b, 3)
                act.wait_ge(pv_done, p * 6 + b + 1)
                act.wait_ge(o_done, p * 6 + b + O_FREE)
                nc.scalar.activation(osum[cols(s, DH), :], ps[DH:P, PVBANK, :], ACT.Copy).then_inc(o_copy, 1)

            def step(kind, p, i, m, before, after):
                own = kind if m > 1 else before
                over = read_out(kind, p, m, before, False)
                if over and own == "B":
                    out_copy(*over)
                if i is None:
                    return
                turned(kind, p, m, 0)
                turned(kind, p, m, 1)
                middle = read_out(kind, p, m, before, True)
                if middle:
                    out_copy(*middle)
                if m + 2 < ITEMS:
                    exps(kind, p, m + 2)
                elif after:
                    exps(after, p + 1, m + 2 - ITEMS)
                if m == V1_AT:
                    values(p, 1)
                if m == V0_AT and after:
                    values(p + 1, 0)
                if over and own == "A":
                    out_copy(*over)
                if m in (2, 3, 4):
                    keys(p, 1, m - 2)
                if m in (5, 6, 7):
                    queries(p, 1, m - 5)
                if m in (11, 12, 13) and after:
                    keys(p + 1, 0, m - 11)
                if m in (14, 15, 16) and after:
                    queries(p + 1, 0, m - 14)

            for g in range(G):
                keys(0, 0, g)
            for g in range(G):
                queries(0, 0, g)
            values(0, 0)
            exps("A", 0, 0)
            exps("A", 0, 1)
            every_pair(act, step)

        def s2_vector(dve):
            def queries_low(p, s, g):
                dve.wait_ge(q_hi[s], p * G + (g + 1))
                v = QS[s][DH:P, cols(g)]
                nc.vector.scalar_tensor_tensor(v, qraw[s][DH:P, cols(g)], -QSCALE, v.bitcast(F32), ALU.mult,
                                               ALU.subtract).then_inc(q_lo[s], 1)

            def table(i, s, part):
                if part < 2:
                    dve.wait_ge(t_ld[s], i * 32 + 32)
                    rows = slice(7 * part, 7 * part + 7)
                    mirrored = bass.AP(tensor=TR, offset=7 * part * GRID + GRID - 1,
                                       ap=[[14 * GRID, P], [GRID, 7], [-1, GRID]])
                    nc.vector.scalar_tensor_tensor(TE[s][:, rows, :], mirrored, -1.0, colmask[:].unsqueeze(1).to_broadcast([P, 7, GRID]),
                                                   ALU.mult, ALU.add).then_inc(tab[s], 1)
                else:
                    dve.wait_ge(tab[s], i * 4 + 2 + TAB_FREE)
                    nc.vector.tensor_copy(TM[s][0:GRID, 0:NA_KH, :], TE[s][0:GRID, 2:2 + NA_KH, :]).then_inc(tab[s], 1)
                    nc.vector.tensor_copy(TM[s][GRID:P, 1:NA_KH + 1, :], TE[s][GRID:P, 3:3 + NA_KH, :]).then_inc(tab[s], 1)

            def values_low(p, s):
                for b in range(2):
                    dve.wait_ge(t_hi[b], fills(p, ("V", s)))
                    nc.vector.tensor_tensor(VT[s][:, 6 * b:6 * b + 6, DH:P], value_src(b),
                                            VT[s][:, 6 * b:6 * b + 6, 0:DH].bitcast(F32), ALU.subtract).then_inc(t_free[b], 1)

            def row_max(kind, p, m):
                s, g, t, _ = item(m)
                _, w, which, r0 = window(kind, m)
                if kind == "A":
                    dve.wait_ge(s_rdy, p * ITEMS + m + 1)
                    nc.vector.tensor_reduce(nmax[:, m:m + 1], score_bank(m, w), AXX, ALU.min).then_inc(m_done, 1)
                else:
                    dve.wait_ge(e_done, p * ITEMS + m - 1)
                    dve.wait_ge(s_rdy, p * ITEMS + m + 1)
                    if m % 12 == 0:
                        dve.wait_ge(tab[s], (p - NPAIR_A) * 4 + 4 + TAB_FREE)
                    dve.sem_inc(dve_passed, 1)
                    table_rows = flat((TM if which == "mid" else TE)[s][:, r0:r0 + w // GRID, :])
                    nc.vector.tensor_tensor_reduce(out=SC[:, m % 2, 0:w], in0=score_bank(m, w), in1=table_rows, scale=1.0,
                                                   scalar=3e38, op0=ALU.add, op1=ALU.min,
                                                   accum_out=nmax[:, m:m + 1]).then_inc(m_done, 1)

            def turned_low(kind, p, m, b):
                _, w, _, _ = window(kind, m)
                dve.wait_ge(t_hi[b], fills(p, ("T", m)))
                nc.vector.tensor_tensor(turned_dst(PTL, m, w, b), turned_src(b, len(split_blocks(w)[b])),
                                        turned_dst(PTH, m, w, b).bitcast(F32), ALU.subtract).then_inc(t_free[b], 1)

            def inverse(p, b):
                dve.wait_ge(e_done, p * ITEMS + 4 * b + 4)
                nc.vector.reciprocal(rinv[:, b % 2, :], rsum[:, 4 * b:4 * b + 4]).then_inc(ri_ok, 1)

            def out(p, b):
                s, g = divmod(b, 3)
                rows = cols(s, DH)
                dve.wait_ge(o_copy, p * 6 + b + 1)
                nc.vector.tensor_tensor(osum[rows, :], ps[0:DH, PVBANK, :], osum[rows, :], ALU.add).then_inc(o_sum, 1)
                dve.wait_ge(o_sum, p * 6 + b + 1)
                dve.wait_ge(r_rdy, p * 6 + b + 1)
                dst = H[rows, bass.ds(p, 1), cols(g)].rearrange("p a n -> p (a n)")
                nc.vector.tensor_tensor(dst, osum[rows, :], ps[rows, RBANK, :], ALU.mult).then_inc(o_done, 1)

            def step(kind, p, i, m, before, after):
                own = kind if m > 1 else before
                over = read_out(kind, p, m, before, False)
                if over and own == "B":
                    out(*over)
                if i is not None:
                    middle = read_out(kind, p, m, before, True)
                    late = own == "B" and m % 4 == 1
                    if late:
                        turned_low(kind, p, m, 0)
                        turned_low(kind, p, m, 1)
                    if middle:
                        out(*middle)
                    if m + 2 < ITEMS:
                        row_max(kind, p, m + 2)
                    elif after:
                        row_max(after, p + 1, m + 2 - ITEMS)
                    if not late:
                        turned_low(kind, p, m, 0)
                        turned_low(kind, p, m, 1)
                    if m % 4 == 2:
                        inverse(p, m // 4)
                    if m == V1_AT:
                        values_low(p, 1)
                    if m == V0_AT and after:
                        values_low(p + 1, 0)
                    if m in (6, 7, 8):
                        queries_low(p, 1, m - 6)
                    if m in (15, 16, 17) and after:
                        queries_low(p + 1, 0, m - 15)
                    if m in (3, 4, 5) and kind == "B":
                        table(i, 1, m - 3)
                    if m in (18, 19, 20) and after == "B":
                        table(0 if kind == "A" else i + 1, 0, m - 18)
                if over and own == "A":
                    out(*over)

            dve.wait_ge(zeroed, 6)
            for g in range(G):
                queries_low(0, 0, g)
            values_low(0, 0)
            row_max("A", 0, 0)
            row_max("A", 0, 1)
            every_pair(dve, step)

        oh_hi, oh_lo, r_free, r_t, r_s, h_up, h_sq, h_acc, acc_zero = (
            sem(x) for x in ("oh_hi", "oh_lo", "r_free", "r_t", "r_s", "h_up", "h_sq", "h_acc", "acc_zero"))
        o_rdy = sem("o_rdy")

        def s3_sync(sp):
            load_weight(sp, OUT0, 0)
            load_weight(sp, OUT0 + 1, 1)
            for k in range(KT):
                sp.wait_ge(oh_lo, (G - 1) * KT + k + 1)
                nc.sync.dma_start(H[:, k, :], a["xT"][cols(k, P), :]).then_inc(x_ld[k], 16)
            with sp.Fori(0, N_OUT // 2) as i:
                load_weight(sp, i * 2 + (OUT0 + 2), 0)
                load_weight(sp, i * 2 + (OUT0 + 3), 1)

        def s3_pool(pool):
            pool.sem_inc(h_acc, 1)
            nc.gpsimd.memset(rstd_h[:], 0.0).then_inc(acc_zero, 1)
            scale_weight(pool, OUT0, 0, 1, OUT0 + 1)
            scale_weight(pool, OUT0 + 1, 1, 1, OUT0 + 2)
            pool.wait_ge(acc_zero, 1)

            def body(i, last=False):
                for second in range(2):
                    if not last:
                        scale_weight(pool, i * 2 + (OUT0 + 2 + second), second, 1, None)
                    for g in range(G):
                        c = i * 6 + (3 * second + g)
                        pool.wait_ge(h_sq, c + 1)
                        pool.wait_ge(h_acc, c + 1)
                        nc.gpsimd.tensor_tensor(rstd_h[:, cols(g)], rstd_h[:, cols(g)], sqh[:, (3 * second + g) % 2, :],
                                                ALU.add).then_inc(h_acc, 1)

            with pool.Fori(0, N_OUT // 2 - 1) as i:
                body(i)
            scale_weight(pool, FF0, 0, 2, None)
            scale_weight(pool, FF0 + 1, 1, 2, None)
            body(N_OUT // 2 - 1, last=True)

        def s3_tensor(pe):
            rms_sums(pe, [(acc_o[0], ones_half, 12), (acc_o[1], ones_half, 12)], 6)
            for b in range(6):
                rms_spread(pe, G + 1, b, G + b + 1, 7 - b % 2, G + b - 1 if b > 1 else None)

            def body(i, first=False):
                for second in range(2):
                    n = i * 2 + (OUT0 + second)
                    pe.wait_ge(w_lo, n + 1)
                    for g in range(G):
                        c = i * 6 + (3 * second + g)
                        if first and second == 0:
                            pe.wait_ge(oh_lo, KT * (g + 1))
                        at_least(pe, r_free, (c - G) * 2 + 2)
                        project(ps[:, 2 * g, :], second, g, range(KT // 2))
                        mm = project(ps[:, 2 * g + 1, :], second, g, range(KT // 2, KT))
                        mm.then_inc(o_rdy if g < 2 else w_done, 1)

            body(0, True)
            with pe.Fori(1, N_OUT // 2) as i:
                body(i)

        def s3_scalar(act):
            rms_std(act, G + 1, 24, 6)
            split_hi(act, OUT0, 0, OUT0 + 1)

            def split(g):
                for k in range(KT):
                    nc.scalar.activation(NH[:, k, cols(g)], H[:, k, cols(g)], ACT.Copy).then_inc(oh_hi, 1)

            split(0)
            for b in range(6):
                half, g = divmod(b, 3)
                rms_row(act, G + b + 1, 7 - b % 2, acc_o[half][:, cols(g)])
            split(1)
            split(2)

            def body(i):
                for second in range(2):
                    n = i * 2 + (OUT0 + second)
                    split_hi(act, n + 1, 1 - second, n + 2)
                    for g in range(G):
                        c = i * 6 + (3 * second + g)
                        act.wait_ge(h_up, c + 1)
                        at_least(act, h_acc, c)
                        src = H[:, bass.ds(i * 2 + second, 1), cols(g)].rearrange("p a n -> p (a n)")
                        nc.scalar.activation(sqh[:, (3 * second + g) % 2, :], src, ACT.Square).then_inc(h_sq, 1)

            body(0)
            with act.Fori(1, N_OUT // 2) as i:
                body(i)

        def s3_vector(dve):
            rms_recip(dve, G + 1, 24)
            split_lo(dve, OUT0, 0)
            for g in range(G):
                for k in range(KT):
                    dve.wait_ge(oh_hi, KT * g + k + 1)
                    nc.vector.tensor_tensor(NL[:, k, cols(g)], H[:, k, cols(g)], NH[:, k, cols(g)].bitcast(F32),
                                            ALU.subtract).then_inc(oh_lo, 1)
            dve.wait_ge(st_ok, G + 6)

            def body(i, first=False):
                for second in range(2):
                    n = i * 2 + (OUT0 + second)
                    split_lo(dve, n + 1, 1 - second)
                    for g in range(G):
                        c = i * 6 + (3 * second + g)
                        if g < 2:
                            dve.wait_ge(o_rdy, i * 4 + (2 * second + g + 1))
                        else:
                            dve.wait_ge(w_done, n + 1)
                        for half in range(2):
                            nc.vector.tensor_tensor(to[:, g % 2, half, :], ps[:, 2 * g + half, :],
                                                    acc_o[half][:, cols(g)], ALU.mult).then_inc(r_free, 1)
                        dve.wait_ge(r_free, c * 2 + 2)
                        nc.vector.tensor_tensor(to[:, g % 2, 0, :], to[:, g % 2, 0, :], to[:, g % 2, 1, :],
                                                ALU.add).then_inc(r_t, 1)
                        if first and g == 0:
                            dve.wait_ge(x_ld[second], 16 * (G + 1))
                        elif g == 0:
                            pass
                        dve.wait_ge(r_t, c + 1)
                        h = H[:, bass.ds(i * 2 + second, 1), cols(g)].rearrange("p a n -> p (a n)")
                        nc.vector.tensor_tensor(h, h, to[:, g % 2, 0, :], ALU.add).then_inc(h_up, 1)

            body(0, True)
            for k in range(2, KT):
                dve.wait_ge(x_ld[k], 16 * (G + 1))
            with dve.Fori(1, N_OUT // 2) as i:
                body(i)

        n_hi, n_lo, u_done, c_ok, tap, gl_ok, mul_ok, m_hi, m_lo, d_rdy, h_add, f_sq, f_acc, f_hi, f_lo, acc_zero2 = (
            sem(x) for x in ("n_hi", "n_lo", "u_done", "c_ok", "tap", "gl_ok", "mul_ok", "m_hi", "m_lo", "d_rdy", "h_add",
                             "f_sq", "f_acc", "f_hi", "f_lo", "acc_zero2"))
        H_FREE = KT * G + 2
        DOWN_BANKS = [(6, 7, 0, 1, 2)[c % 5] if c < 20 else 6 + c % 2 for c in range(KT * G)]
        CALL4, ROW4 = G + 2, G + 6
        NTILE = KT * G

        def first_tile(j):
            return j * 3 + (FF0 - 1)

        def in_pairs(eng, body):
            with eng.Fori(0, (NJ - 2) // 2) as q:
                body(q * 2 + 1, 0)
                body(q * 2 + 2, 1)
            body(NJ - 1, 0)

        def s4_sync(sp):
            with sp.Fori(0, (N_FF - 2) // 2) as i:
                load_weight(sp, i * 2 + (FF0 + 2), 0)
                load_weight(sp, i * 2 + (FF0 + 3), 1)
            load_weight(sp, PLE0, 0)
            load_weight(sp, PLE0 + 1, 1)
            sp.wait_ge(u_done, 2 * NJ)
            nc.sync.dma_start(rstd_h[:], a["pT"][0:P, :]).then_inc(p_ld, 16)

        def s4_pool(pool):
            pool.sem_inc(h_add, H_FREE)
            pool.sem_inc(mul_ok, 1)

            def body(j, odd):
                n = first_tile(j)
                scale_weight(pool, n, odd, 2, None)
                scale_weight(pool, n + 1, 1 - odd, 2, None)

            in_pairs(pool, body)
            pool.wait_ge(mul_ok, NJ + 1)
            nc.gpsimd.memset(acc_h[:], 0.0).then_inc(acc_zero2, 1)
            pool.wait_ge(acc_zero2, 1)
            for c in range(NTILE):
                g = c % G
                pool.wait_ge(f_sq, c + 1)
                at_least(pool, f_acc, c)
                nc.gpsimd.tensor_tensor(acc_h[:, cols(g)], acc_h[:, cols(g)], sqd[:, c % 2, :], ALU.add).then_inc(f_acc, 1)

        def s4_tensor(pe):
            rms_sums(pe, [(rstd_h, ones_d, 12)], 6)
            for b in range(G):
                rms_spread(pe, CALL4, b, ROW4 + b + 1, 7 - b % 2, ROW4 + 1 if b == 2 else None)

            def up(n, slot, bank, freed, first=False):
                pe.wait_ge(w_lo, n + 1)
                at_least(pe, u_done, freed)
                for g in range(G):
                    if first:
                        pe.wait_ge(n_lo, KT * (g + 1))
                    mm = project(ps[:, bank + g, :], slot, g)
                mm.then_inc(w_done, 1)

            def down(n, slot, j, last=False):
                pe.wait_ge(w_lo, n + 1)
                pe.wait_ge(m_lo, j + 1)
                for c in range(NTILE):
                    m, g = divmod(c, G)
                    bank = DOWN_BANKS[c]
                    before = [x for x in range(c) if DOWN_BANKS[x] == bank]
                    if before or bank >= 6:
                        pe.wait_ge(h_add, j * NTILE + (before[-1] + 1 + H_FREE if before else H_FREE))
                    else:
                        pe.wait_ge(u_done, 2 * NJ if last else j * 2 + 3)
                    mm = three_pass(ps[:, bank, :], WH[:, slot, cols(m, P)], WL[:, slot, cols(m, P)], MH[:, cols(g)],
                                    ML[:, cols(g)], True, True)
                    mm.then_inc(d_rdy if c < NTILE - 1 else w_done, 1)

            up(FF0, 0, 0, 0, True)
            up(FF0 + 1, 1, 3, 0)
            pe.wait_ge(st_ok, ROW4 + G)

            def body(j, odd):
                n = first_tile(j)
                pe.wait_ge(h_add, (j - 2) * NTILE + (20 + H_FREE))
                up(n, odd, 0, j * 2 - 1)
                up(n + 1, 1 - odd, 3, j * 2)
                down(n + 2, odd, j - 1)

            in_pairs(pe, body)
            down(PLE0 - 1, 1, NJ - 1, True)

        def s4_scalar(act):
            rms_std(act, CALL4, 12, 6)
            for g in range(G):
                for k in range(KT):
                    nc.scalar.activation(NH[:, k, cols(g)], H[:, k, cols(g)], ACT.Copy).then_inc(n_hi, 1)
                if g == 0:
                    for b in range(G):
                        rms_row(act, ROW4 + b + 1, 7 - b % 2, rstd_h[:, cols(b)])

            def centre(j, gate):
                act.wait_ge(u_done, j * 2 + 1 + gate)
                f = j + NJ * gate
                if gate:
                    act.wait_ge(mul_ok, j + 1)
                else:
                    at_least(act, m_lo, j)
                nc.scalar.activation((cg if gate else ca)[:], u[:], ACT.Identity, bias=convb[:, bass.ds(f, 1)],
                                     scale=convw[:, bass.ds(f, 1), 1:2].rearrange("p a b -> p (a b)")).then_inc(c_ok, 1)

            def gate_out(j):
                centre(j, 1)
                act.wait_ge(tap, j * 8 + 8)
                nc.scalar.activation(cg[:], cg[:], ACT.Gelu_apprx_tanh).then_inc(gl_ok, 1)
                act.wait_ge(mul_ok, j + 2)
                if isinstance(j, int) and j == NJ - 1:
                    act.wait_ge(w_done, PLE0 - 1)
                else:
                    act.wait_ge(w_done, first_tile(j + 1))
                nc.scalar.activation(MH[:], ca[:], ACT.Copy).then_inc(m_hi, 1)

            split_hi(act, FF0 + 1, 1, FF0 + 2)
            split_hi(act, FF0 + 2, 0, FF0 + 3)
            centre(0, 0)

            def body(j, odd, last=False):
                n = first_tile(j)
                scaled = FF0 + 1 + j * 2
                split_hi(act, n + 1, 1 - odd, scaled + 1)
                gate_out(j - 1)
                split_hi(act, n + 2, odd, None)
                centre(j, 0)
                split_hi(act, n + 3, 1 - odd, None if last else scaled + 2)

            with act.Fori(0, (NJ - 2) // 2) as q:
                body(q * 2 + 1, 0)
                body(q * 2 + 2, 1)
            body(NJ - 1, 0, True)
            split_hi(act, PLE0, 0, None)
            gate_out(NJ - 1)
            act.wait_ge(m_lo, NJ)
            for c in range(NTILE):
                m, g = divmod(c, G)
                act.wait_ge(h_add, (NJ - 1) * NTILE + c + 1 + H_FREE)
                nc.scalar.activation(NH[:, m, cols(g)], H[:, m, cols(g)], ACT.Copy).then_inc(f_hi, 1)
                at_least(act, f_acc, c - 1)
                nc.scalar.activation(sqd[:, c % 2, :], H[:, m, cols(g)], ACT.Square).then_inc(f_sq, 1)

        def s4_vector(dve):
            rms_recip(dve, CALL4, 12)
            for g in range(G):
                for k in range(KT):
                    dve.wait_ge(n_hi, KT * g + k + 1)
                    nc.vector.tensor_tensor(NL[:, k, cols(g)], H[:, k, cols(g)], NH[:, k, cols(g)].bitcast(F32),
                                            ALU.subtract).then_inc(n_lo, 1)

            def taps(j, gate, n):
                dve.wait_ge(w_done, n + 1)
                at_least(dve, tap, j * 8 + 4 * gate)
                nc.vector.tensor_tensor(u[:], flat(ps[:, 3 * gate:3 * gate + 3, :]), rstd_h[:], ALU.mult).then_inc(u_done, 1)
                dve.wait_ge(c_ok, j * 2 + 1 + gate)
                f = j + NJ * gate
                buf = cg if gate else ca
                t0 = j * 8 + 4 * gate
                for x, (w, to_, from_) in enumerate((
                        (0, slice(1, TP), slice(0, TP - 1)), (0, slice(TP + 1, T), slice(TP, T - 1)),
                        (2, slice(0, TP - 1), slice(1, TP)), (2, slice(TP, T - 1), slice(TP + 1, T)))):
                    if x > 1:
                        dve.wait_ge(tap, t0 + x - 1)
                    nc.vector.scalar_tensor_tensor(buf[:, to_], u[:, from_], convw[:, bass.ds(f, 1), w:w + 1].rearrange("p a b -> p (a b)"),
                                                   buf[:, to_], ALU.mult, ALU.add).then_inc(tap, 1)

            def gate_out(j, n):
                taps(j, 1, n)
                dve.wait_ge(gl_ok, j + 1)
                nc.vector.tensor_tensor(ca[:], ca[:], cg[:], ALU.mult).then_inc(mul_ok, 1)
                dve.wait_ge(m_hi, j + 1)
                nc.vector.tensor_tensor(ML[:], ca[:], MH[:].bitcast(F32), ALU.subtract).then_inc(m_lo, 1)

            def add_down(j, n, extra=False, split_next=None):
                for c in range(NTILE):
                    m, g = divmod(c, G)
                    if c < NTILE - 1:
                        dve.wait_ge(d_rdy, j * (NTILE - 1) + (c + 1))
                    else:
                        dve.wait_ge(w_done, n + 1)
                    h = H[:, m, cols(g)]
                    nc.vector.tensor_tensor(h, h, ps[:, DOWN_BANKS[c], :], ALU.add).then_inc(h_add, 1)
                    if c == 3 and split_next:
                        split_lo(dve, *split_next)
                    if extra and c:
                        rest(c - 1)
                if extra:
                    rest(NTILE - 1)

            def rest(c):
                m, g = divmod(c, G)
                dve.wait_ge(f_hi, c + 1)
                nc.vector.tensor_tensor(NL[:, m, cols(g)], H[:, m, cols(g)], NH[:, m, cols(g)].bitcast(F32),
                                        ALU.subtract).then_inc(f_lo, 1)

            dve.wait_ge(st_ok, ROW4 + G)
            split_lo(dve, FF0 + 1, 1)
            split_lo(dve, FF0 + 2, 0)
            taps(0, 0, FF0)

            def body(j, odd):
                n = first_tile(j)
                split_lo(dve, n + 1, 1 - odd)
                if isinstance(j, int) and j == 1:
                    gate_out(0, FF0 + 1)
                else:
                    gate_out(j - 1, n - 2 if not isinstance(j, int) or j > 1 else FF0 + 1)
                split_lo(dve, n + 2, odd)
                taps(j, 0, n)
                add_down(j - 1, n + 2, split_next=(n + 3, 1 - odd))

            in_pairs(dve, body)
            split_lo(dve, PLE0, 0)
            gate_out(NJ - 1, first_tile(NJ - 1) + 1)
            add_down(NJ - 1, PLE0 - 1, True)

        CALL5, ROW5 = CALL4 + 1, ROW4 + G
        CALL6, ROW6 = CALL5 + 1, ROW5 + G
        acc_zero3, pl_rdy, gt_rdy, g_t, g_sig, g_mul, g_up, g_sq, g_acc, y_ok = (
            sem(x) for x in ("acc_zero3", "pl_rdy", "gt_rdy", "g_t", "g_sig", "g_mul", "g_up", "g_sq", "g_acc", "y_ok"))
        UP_FREE, ACC_FREE = 6, 2
        NQ = KT // 2
        SCALED4 = FF0 + 2 * NJ

        def in_halves(eng, body):
            with eng.Fori(0, NQ // 2) as r:
                body(r * 2, 0)
                body(r * 2 + 1, 1)

        def s5_sync(sp):
            sp.wait_ge(p_lo, 1)
            nc.sync.dma_start(rstd_h[:], a["pT"][P:2 * P, :]).then_inc(p_ld, 16)
            with sp.Fori(0, (N_PLE - 2) // 2) as i:
                load_weight(sp, i * 2 + (PLE0 + 2), 0)
                load_weight(sp, i * 2 + (PLE0 + 3), 1)
            load_weight(sp, NW, 0)
            for k in range(KT):
                sp.wait_ge(y_ok, k + 1)
                nc.sync.dma_start(a["yT"][cols(k, P), :], H[:, k, :]).then_inc(stored, 16)
            sp.wait_ge(stored, 16 * KT)
            sp.wait_ge(w_ld[0], landed(NW, 0))

        def s5_pool(pool):
            pool.sem_inc(g_up, UP_FREE)
            pool.sem_inc(g_acc, ACC_FREE)
            pool.wait_ge(st_mm, CALL5)
            nc.gpsimd.memset(acc_h[:], 0.0).then_inc(acc_zero3, 1)

            def body(q, odd):
                n = q * 3 + PLE0
                scale_weight(pool, n + 1, 1 - odd, 3, None)
                scale_weight(pool, n + 2, odd, 3, None)

            in_halves(pool, body)

        def s5_tensor(pe):
            rms_sums(pe, [(acc_h, ones_d, 12)], 6)
            for b in range(G):
                rms_spread(pe, CALL5, b, ROW5 + b + 1, 7 - b % 2, ROW5 + 1 if b == 2 else None)
            pe.wait_ge(p_lo, 2)
            pe.wait_ge(st_ok, ROW5 + G)

            def body(q, odd):
                n = q * 3 + PLE0
                pe.wait_ge(w_lo, n + 1)
                for c in range(6):
                    mm_, g = divmod(c, G)
                    pe.wait_ge(g_up, q * 6 + (c + 1))
                    for k in range(2):
                        w = cols(2 * mm_ + k, P)
                        mm = three_pass(ps[:, c, :], WH[:, odd, w], WL[:, odd, w], PH[:, k, cols(g)], PL[:, k, cols(g)],
                                        k == 0, k == 1)
                    mm.then_inc(pl_rdy if c < 5 else w_done, 1)
                for second in range(2):
                    slot = (odd + 1 + second) % 2
                    pe.wait_ge(w_lo, n + 2 + second)
                    for g in range(G):
                        c = 3 * second + g
                        pe.wait_ge(g_acc, q * 6 + (c - 2 + 1 + ACC_FREE))
                        mm = project(ps[:, 6 + c % 2, :], slot, g)
                        mm.then_inc(gt_rdy if g < 2 else w_done, 1)

            in_halves(pe, body)
            pe.wait_ge(g_acc, NQ * 6 + ACC_FREE)
            rms_sums(pe, [(acc_h, ones_d, 12)], 0)
            for b in range(G):
                rms_spread(pe, CALL6, b, ROW6 + b + 1, 1 + b)

        def s5_scalar(act):
            act.wait_ge(p_ld, 16)
            nc.scalar.activation(PH[:, 0, :], rstd_h[:], ACT.Copy).then_inc(p_hi, 1)
            rms_std(act, CALL5, 12, 6)
            act.wait_ge(p_ld, 32)
            nc.scalar.activation(PH[:, 1, :], rstd_h[:], ACT.Copy).then_inc(p_hi, 1)
            act.wait_ge(p_lo, 2)
            for b in range(G):
                rms_row(act, ROW5 + b + 1, 7 - b % 2, rstd_h[:, cols(b)])

            def body(q, odd):
                n = q * 3 + PLE0
                split_hi(act, n + 1, 1 - odd, q * 2 + (SCALED4 + 1))
                for second in range(2):
                    slot = (odd + second) % 2
                    split_hi(act, n + 2 + second, slot, q * 2 + (SCALED4 + 2) if second == 0 else None)
                    for g in range(G):
                        c = 3 * second + g
                        act.wait_ge(g_t, q * 6 + (c + 1))
                        nc.scalar.activation(gate_t[:], gate_t[:], ACT.Sigmoid).then_inc(g_sig, 1)
                        act.wait_ge(g_up, q * 6 + (c + 1 + UP_FREE))
                        src = H[:, bass.ds(q * 2 + second, 1), cols(g)].rearrange("p a n -> p (a n)")
                        nc.scalar.activation(ps[:, 6 + c % 2, :], src, ACT.Square).then_inc(g_sq, 1)

            in_halves(act, body)
            rms_std(act, CALL6, 12, 0)
            for b in range(G):
                rms_row(act, ROW6 + b + 1, 1 + b, rstd_h[:, cols(b)])

        def s5_vector(dve):
            def p_low(k):
                dve.wait_ge(p_hi, k + 1)
                nc.vector.tensor_tensor(PL[:, k, :], rstd_h[:], PH[:, k, :].bitcast(F32), ALU.subtract).then_inc(p_lo, 1)

            p_low(0)
            rms_recip(dve, CALL5, 12)
            p_low(1)
            dve.wait_ge(st_ok, ROW5 + G)
            dve.wait_ge(acc_zero3, 1)

            def body(q, odd):
                n = q * 3 + PLE0
                split_lo(dve, n + 1, 1 - odd)
                for second in range(2):
                    split_lo(dve, n + 2 + second, (odd + second) % 2)
                    for g in range(G):
                        c = 3 * second + g
                        if g < 2:
                            dve.wait_ge(gt_rdy, q * 4 + (2 * second + g + 1))
                        else:
                            dve.wait_ge(w_done, n + 2 + second)
                        bank = ps[:, 6 + c % 2, :]
                        nc.vector.tensor_tensor(gate_t[:], bank, rstd_h[:, cols(g)], ALU.mult).then_inc(g_t, 1)
                        dve.wait_ge(g_sig, q * 6 + (c + 1))
                        if c < 3:
                            dve.wait_ge(w_done, n + 1)
                        nc.vector.tensor_tensor(gate_t[:], gate_t[:], ps[:, c, :], ALU.mult).then_inc(g_mul, 1)
                        dve.wait_ge(g_mul, q * 6 + (c + 1))
                        h = H[:, bass.ds(q * 2 + second, 1), cols(g)].rearrange("p a n -> p (a n)")
                        nc.vector.tensor_tensor(h, h, gate_t[:], ALU.add).then_inc(g_up, 1)
                        dve.wait_ge(g_sq, q * 6 + (c + 1))
                        nc.vector.tensor_tensor(acc_h[:, cols(g)], acc_h[:, cols(g)], bank, ALU.add).then_inc(g_acc, 1)

            in_halves(dve, body)
            rms_recip(dve, CALL6, 12)
            dve.wait_ge(st_ok, ROW6 + G)
            for k in range(KT):
                nc.vector.scalar_tensor_tensor(H[:, k, :], H[:, k, :], final_g[:, k:k + 1], rstd_h[:], ALU.mult,
                                               ALU.mult).then_inc(y_ok, 1)

        p_ld, p_hi, p_lo = sem("p_ld"), sem("p_hi"), sem("p_lo")
        block = ctx.enter_context(nc.Block())

        @block.sync
        def _(sp):
            s1_sync(sp)
            end_stage(sp, 0)
            s2_sync(sp)
            end_stage(sp, 1)
            s3_sync(sp)
            end_stage(sp, 2)
            s4_sync(sp)
            end_stage(sp, 3)
            s5_sync(sp)

        @block.gpsimd
        def _(pool):
            s1_pool(pool)
            end_stage(pool, 0)
            s2_pool(pool)
            end_stage(pool, 1)
            s3_pool(pool)
            end_stage(pool, 2)
            s4_pool(pool)
            end_stage(pool, 3)
            s5_pool(pool)

        @block.tensor
        def _(pe):
            s1_tensor(pe)
            end_stage(pe, 0)
            s2_tensor(pe)
            end_stage(pe, 1)
            s3_tensor(pe)
            end_stage(pe, 2)
            s4_tensor(pe)
            end_stage(pe, 3)
            s5_tensor(pe)

        @block.scalar
        def _(act):
            s1_scalar(act)
            end_stage(act, 0)
            s2_scalar(act)
            end_stage(act, 1)
            s3_scalar(act)
            end_stage(act, 2)
            s4_scalar(act)
            end_stage(act, 3)
            s5_scalar(act)

        @block.vector
        def _(dve):
            s1_vector(dve)
            end_stage(dve, 0)
            s2_vector(dve)
            end_stage(dve, 1)
            s3_vector(dve)
            end_stage(dve, 2)
            s4_vector(dve)
            end_stage(dve, 3)
            s5_vector(dve)


def shape_constants():
    f = np.float32
    k = np.arange(P)
    out = {"ident": np.eye(P, dtype=f), "ones_d": np.full((P, 1), 1.0 / D, f),
           "ones_half": np.full((P, 1), 2.0 / D, f), "eps": np.full((P, 1), EPS, f),
           "blk": np.where(k[:, None] // DH == k[None, :] // DH, f(1.0 / DH), f(0)).astype(f)}
    perm = np.zeros((P, P), f)
    first = k[k % 32 < 16]
    perm[first + 16, first] = -1.0
    perm[first, first + 16] = 1.0
    out["perm"] = perm
    t = np.arange(TS)
    freqs = (10000.0 ** (-np.arange(0, DH // 2, 2, dtype=f) / f(DH // 2))).astype(f)
    pos = np.where((k[:, None] % DH) < DH // 2, (t // GRID)[None, :], (t % GRID)[None, :]).astype(f)
    ang = pos * freqs[k % 16][:, None]
    out["rope_c"], out["rope_s"] = np.cos(ang).astype(f), np.sin(ang).astype(f)
    c = k[:, None] % GRID
    start = np.clip(c - NA_KW // 2, 0, GRID - NA_KW)
    kc = np.arange(GRID)[None, :]
    out["colmask"] = np.where((kc >= start) & (kc < start + NA_KW), f(0), f(NEG)).astype(f)
    return out


def layout(x):
    def cat_t(p, s):
        return np.concatenate([p.reshape(-1, p.shape[-1]), s.reshape(-1, s.shape[-1])], 0).T

    def feature_rows(v):
        return v.reshape(-1, P).T

    def tile(w, columns):
        return w[:, columns].reshape(-1, P, P).transpose(1, 0, 2).reshape(P, -1)

    w_in, w_out, w_up = x["w_in"][0], x["w_out"][0], x["w_up"][0]
    w_down, w_gate, w_ple = x["w_down"][0], x["w_ple_gate"][0], x["w_ple"][0]
    pair = np.concatenate([np.concatenate([np.arange(DH) + DH * i, np.arange(DH) + DH * (i + 4)]) for i in range(4)])
    k = np.arange(P)
    head = [pair[:P], pair[P:2 * P], pair[2 * P:3 * P], pair[3 * P:], 512 + k]
    plain = [640 + k] + [768 + 512 * part + P * i + k for i in range(4) for part in range(3)]
    order = [y for two in zip(head, plain[:NA_TILES]) for y in two] + plain[NA_TILES:]
    rows = np.concatenate([pair, 512 + np.arange(512)])
    tiles = [tile(w_in, q) for q in order]
    tiles += [tile(w_out[rows], P * m + k) for m in range(KT)]

    def up(j, gate):
        return tile(w_up, FF * gate + P * j + k)

    tiles += [up(0, 0), up(0, 1)]
    for j in range(1, NJ):
        tiles += [up(j, 0), up(j, 1), w_down[P * (j - 1):P * j]]
    tiles.append(w_down[P * (NJ - 1):])
    for q in range(4):
        both = np.concatenate([tile(w_ple, P * (2 * q + m) + k) for m in range(2)], 1)
        tiles += [np.pad(both, ((0, 0), (0, D - both.shape[1]))), tile(w_gate, P * 2 * q + k), tile(w_gate, P * (2 * q + 1) + k)]
    tiles.append(np.zeros((P, D), np.float32))
    conv = x["conv_w"][0].reshape(3, 2 * NJ, P).transpose(2, 1, 0).reshape(P, -1)
    o_gain = np.concatenate([x["out_norm_a"][0][pair], x["out_norm_b"][0]])
    gains = np.concatenate([feature_rows(x["attn_norm"][0]), feature_rows(o_gain), feature_rows(x["ffn_norm"][0]),
                            feature_rows(x["ple_norm"][0])], 1)
    qg = np.concatenate([x["q_norm_a"][0]] * 2)[:, None]
    kg = np.concatenate([x["k_norm_a"][0]] * 2)[:, None]
    arrays = {"w": np.stack(tiles), "xT": cat_t(x["x_prompt"], x["x_sample"]), "pT": cat_t(x["p_prompt"][0], x["p_sample"][0]),
              "gains": gains, "final_g": feature_rows(x["final_norm"]), "qk_g": np.concatenate([qg] * 4 + [kg], 1),
              "convw": conv, "convb": feature_rows(x["conv_b"][0]), "rpb": np.pad(x["rpb_b"][0][:, :, ::-1].reshape(-1), RPB_PAD)[None, :]}
    arrays.update(shape_constants())
    return {n: np.ascontiguousarray(v) for n, v in arrays.items()}


def program(nc, arrays):
    a = {}
    for name, v in arrays.items():
        h = nc.dram_tensor(f"in_{name}", v.shape, mybir.dt.from_np(v.dtype), kind="ExternalInput")
        a[name] = h.ap()
        if name == "rpb":
            a["rpb_tensor"] = h
    a["qkv"] = nc.dram_tensor("qkv", (N_IN, P, T), F32, kind="Internal").ap()
    a["yT"] = nc.dram_tensor("out_yT", (D, T), F32, kind="ExternalOutput").ap()
    build(nc, a)


def kernel(**inputs):
    import concourse.bacc as bacc
    from concourse.bass_utils import run_bass_kernel_spmd

    arrays = layout({n: np.asarray(v) for n, v in inputs.items()})
    nc = bacc.Bacc("TRN2", target_bir_lowering=False, num_devices=1)
    program(nc, arrays)
    r = run_bass_kernel_spmd(nc, [{f"in_{n}": v for n, v in arrays.items()}], core_ids=[0])
    y = r.results[0]["out_yT"]
    return (np.ascontiguousarray(y[:, :TP].T)[None], np.ascontiguousarray(y[:, TP:].T)[None])
```
